# Optimizing a Trainium2 kernel written in Bass

```python
import jax, jax.numpy as jnp
from jax import lax
import numpy as np

D_MODEL = 1024
BATCH = 1
SEQ = 256
DEPTH = 2

GRID_W = 64
CTX_LEN = 256
HEAD_DIM = 64
Q_BLOCK = 128
ROPE_THETA = 10000.0
EPS = 1e-6
M_INIT = -1e30
M_HEADS = 4
M_HEAD_DIM = 128
M_WIDTH = M_HEADS * M_HEAD_DIM
M_CHUNK = 128
CONV_K = 3
G_HEADS = 8
G_KV_HEADS = 2
W_HEADS = 8
W_KV_HEADS = 2
WINDOW = 128
N_HEADS = 8
NB_ROWS = 8
NB_COLS = 16
N_BRANCH = 4
BRANCH_WIDTH = 512
N_EXPERTS = 32
N_GROUPS = 4
EXPERTS_PER_GROUP = N_EXPERTS // N_GROUPS
TOP_K = 2
D_EXPERT = 512
MOE_BLOCK = 128
PROJ_WIDTHS = (M_WIDTH, M_WIDTH, M_WIDTH, M_WIDTH, 4 * M_HEADS,
               G_HEADS * HEAD_DIM, G_KV_HEADS * HEAD_DIM, G_KV_HEADS * HEAD_DIM,
               W_HEADS * HEAD_DIM, W_KV_HEADS * HEAD_DIM, W_KV_HEADS * HEAD_DIM,
               N_HEADS * HEAD_DIM, N_HEADS * HEAD_DIM, N_HEADS * HEAD_DIM,
               N_BRANCH * D_MODEL)
N_PROJ = sum(PROJ_WIDTHS)

kernel_name = 'hybrid_mlstm_gqa_swa_natten_moe_dit_block'

def rms_norm(x, g):
    xf = x.astype(jnp.float32)
    y = xf * lax.rsqrt(jnp.mean(xf * xf, axis=-1, keepdims=True) + EPS)
    return y.astype(x.dtype) * g

def split_projection(p):
    idx, acc = [], 0
    for w in PROJ_WIDTHS[:-1]:
        acc += w
        idx.append(acc)
    return jnp.split(p, idx, axis=-1)

def to_heads(a, n_heads):
    return a.reshape(a.shape[0], a.shape[1], n_heads, HEAD_DIM)

def axial_rope_tables(n_tokens):
    t = jnp.arange(n_tokens, dtype=jnp.int32)
    row = (t // GRID_W).astype(jnp.float32)
    col = (t % GRID_W).astype(jnp.float32)
    n_freq = HEAD_DIM // 4
    inv_freq = ROPE_THETA ** (-jnp.arange(n_freq, dtype=jnp.float32) / n_freq)
    ang = jnp.concatenate([row[:, None] * inv_freq, col[:, None] * inv_freq], axis=-1)
    return jnp.cos(ang), jnp.sin(ang)

def apply_rope(x, cos, sin):
    shp = x.shape
    xf = x.astype(jnp.float32).reshape(shp[:-1] + (shp[-1] // 2, 2))
    x0, x1 = xf[..., 0], xf[..., 1]
    c = cos[None, :, None, :]
    s = sin[None, :, None, :]
    out = jnp.stack([x0 * c - x1 * s, x0 * s + x1 * c], axis=-1)
    return out.reshape(shp).astype(x.dtype)

def ctx_attention(q, k, v, sink=None):
    B, C, Hq, d = q.shape
    Hkv = k.shape[2]
    R = Hq // Hkv
    qg = q.reshape(B, C, Hkv, R, d)
    s = jnp.einsum('bqgrd,bkgd->bgrqk', qg, k).astype(jnp.float32) * d ** -0.5
    if sink is not None:
        sink_col = jnp.broadcast_to(sink.astype(jnp.float32).reshape(1, Hkv, R, 1, 1), (B, Hkv, R, C, 1))
        s = jnp.concatenate([s, sink_col], axis=-1)
    p = jax.nn.softmax(s, axis=-1)[..., :C].astype(v.dtype)
    return jnp.einsum('bgrqk,bkgd->bqgrd', p, v).reshape(B, C, Hq, d)

def global_attention(q, k_all, v_all):
    B, S, Hq, d = q.shape
    Hkv = k_all.shape[2]
    R = Hq // Hkv
    nb = S // Q_BLOCK
    qb = jnp.moveaxis(q.reshape(B, nb, Q_BLOCK, Hkv, R, d), 1, 0)

    def block(qi):
        s = jnp.einsum('bqgrd,bkgd->bgrqk', qi, k_all).astype(jnp.float32) * d ** -0.5
        p = jax.nn.softmax(s, axis=-1).astype(v_all.dtype)
        return jnp.einsum('bgrqk,bkgd->bqgrd', p, v_all)

    o = lax.map(block, qb)
    return jnp.moveaxis(o, 0, 1).reshape(B, S, Hq, d)

def window_attention(q, k, v, kc, vc, sink):
    B, S, Hq, d = q.shape
    Hkv = k.shape[2]
    R = Hq // Hkv
    C = kc.shape[1]
    nb = S // Q_BLOCK
    span = Q_BLOCK + 2 * WINDOW
    pad = ((0, 0), (WINDOW, WINDOW), (0, 0), (0, 0))
    kp = jnp.pad(k, pad)
    vp = jnp.pad(v, pad)
    qb = jnp.moveaxis(q.reshape(B, nb, Q_BLOCK, Hkv, R, d), 1, 0)
    sink_col = jnp.broadcast_to(sink.astype(jnp.float32).reshape(1, Hkv, R, 1, 1), (B, Hkv, R, Q_BLOCK, 1))
    scale = d ** -0.5

    def block(args):
        qi, i = args
        start = i * Q_BLOCK
        ks = lax.dynamic_slice_in_dim(kp, start, span, axis=1)
        vs = lax.dynamic_slice_in_dim(vp, start, span, axis=1)
        qpos = start + jnp.arange(Q_BLOCK)
        kpos = start - WINDOW + jnp.arange(span)
        valid = (jnp.abs(kpos[None, :] - qpos[:, None]) <= WINDOW) & (kpos >= 0)[None, :] & (kpos < S)[None, :]
        s_loc = jnp.einsum('bqgrd,bkgd->bgrqk', qi, ks).astype(jnp.float32) * scale
        s_loc = jnp.where(valid, s_loc, -jnp.inf)
        s_ctx = jnp.einsum('bqgrd,bcgd->bgrqc', qi, kc).astype(jnp.float32) * scale
        p = jax.nn.softmax(jnp.concatenate([s_loc, s_ctx, sink_col], axis=-1), axis=-1).astype(v.dtype)
        return (jnp.einsum('bgrqk,bkgd->bqgrd', p[..., :span], vs)
                + jnp.einsum('bgrqc,bcgd->bqgrd', p[..., span:span + C], vc))

    o = lax.map(block, (qb, jnp.arange(nb)))
    return jnp.moveaxis(o, 0, 1).reshape(B, S, Hq, d)

def neighbourhood_attention(q, k, v, kc, vc, rel_bias):
    B, S, H, d = q.shape
    rows = S // GRID_W
    kh = min(NB_ROWS, rows)
    scale = d ** -0.5
    qg = jnp.moveaxis(q.reshape(B, rows, GRID_W, H, d), 1, 0)
    kg = k.reshape(B, rows, GRID_W, H, d)
    vg = v.reshape(B, rows, GRID_W, H, d)
    col = np.arange(GRID_W)
    col_start = np.clip(col - NB_COLS // 2, 0, GRID_W - NB_COLS)
    col_idx = col_start[:, None] + np.arange(NB_COLS)[None, :]
    dcol = col_idx - col[:, None]
    bias_cols = rel_bias[:, :, dcol + NB_COLS - 1]
    n_loc = kh * NB_COLS

    def block(args):
        qr, r = args
        r0 = jnp.clip(r - kh // 2, 0, rows - kh)
        ks = lax.dynamic_slice_in_dim(kg, r0, kh, axis=1)[:, :, col_idx]
        vs = lax.dynamic_slice_in_dim(vg, r0, kh, axis=1)[:, :, col_idx]
        drow = r0 + jnp.arange(kh) - r
        bias = jnp.moveaxis(bias_cols[:, drow + NB_ROWS - 1], 1, 2)
        s_loc = jnp.einsum('bqhd,bkqjhd->bhqkj', qr, ks).astype(jnp.float32) * scale + bias.astype(jnp.float32)
        s_loc = s_loc.reshape(B, H, GRID_W, n_loc)
        s_ctx = jnp.einsum('bqhd,bchd->bhqc', qr, kc).astype(jnp.float32) * scale
        p = jax.nn.softmax(jnp.concatenate([s_loc, s_ctx], axis=-1), axis=-1).astype(v.dtype)
        p_loc = p[..., :n_loc].reshape(B, H, GRID_W, kh, NB_COLS)
        return (jnp.einsum('bhqkj,bkqjhd->bqhd', p_loc, vs)
                + jnp.einsum('bhqc,bchd->bqhd', p[..., n_loc:], vc))

    o = lax.map(block, (qg, jnp.arange(rows)))
    return jnp.moveaxis(o, 0, 1).reshape(B, S, H, d)

def short_conv(x, w, b):
    y = lax.conv_general_dilated(x, w[:, None, :].astype(x.dtype), window_strides=(1,),
                                 padding=[(CONV_K // 2, CONV_K // 2)],
                                 dimension_numbers=('NWC', 'WIO', 'NWC'),
                                 feature_group_count=x.shape[-1])
    return y + b

def mlstm_inputs(q_raw, k_raw, v_raw, if_raw, conv_w, conv_b, gate_b):
    qk = jax.nn.silu(short_conv(jnp.concatenate([q_raw, k_raw], axis=-1), conv_w, conv_b))
    q, k = jnp.split(qk, 2, axis=-1)
    B, T, _ = q.shape

    def heads(a):
        return jnp.swapaxes(a.reshape(B, T, M_HEADS, M_HEAD_DIM), 1, 2).astype(jnp.float32)

    g = (if_raw.reshape(B, T, 2, 2, M_HEADS) + gate_b).astype(jnp.float32)
    g = jnp.transpose(g, (2, 3, 0, 4, 1))
    log_i = g[:, 0]
    log_f = jax.nn.log_sigmoid(g[:, 1])
    return heads(q), heads(k) * M_HEAD_DIM ** -0.5, heads(v_raw), log_i, log_f

def mlstm_chunk_scan(q, k, v, log_i, log_f, state):
    B, H, T, _ = q.shape
    dv = v.shape[-1]
    L = M_CHUNK
    nc = T // L

    def chunks(a):
        return jnp.moveaxis(a.reshape((B, H, nc, L) + a.shape[3:]), 2, 0)

    tril = jnp.tril(jnp.ones((L, L), dtype=bool))

    def step(carry, xs):
        C, n, m = carry
        qc, kc, vc, ic, fc = xs
        b = jnp.cumsum(fc, axis=-1)
        dmat = jnp.where(tril, b[..., :, None] - b[..., None, :] + ic[..., None, :], -jnp.inf)
        m_inter = b + m[..., None]
        m_t = jnp.maximum(dmat.max(axis=-1), m_inter)
        a = jnp.einsum('bhtd,bhsd->bhts', qc, kc) * jnp.exp(dmat - m_t[..., None])
        inter = jnp.exp(m_inter - m_t)
        num = jnp.einsum('bhts,bhsv->bhtv', a, vc) + inter[..., None] * jnp.einsum('bhtd,bhdv->bhtv', qc, C)
        den = a.sum(axis=-1) + inter * jnp.einsum('bhtd,bhd->bht', qc, n)
        h = num / jnp.maximum(jnp.abs(den), jnp.exp(-m_t))[..., None]
        b_end = b[..., -1]
        g = b_end[..., None] - b + ic
        m_new = jnp.maximum(b_end + m, g.max(axis=-1))
        decay = jnp.exp(b_end + m - m_new)
        wg = jnp.exp(g - m_new[..., None])
        C_new = decay[..., None, None] * C + jnp.einsum('bhs,bhsd,bhsv->bhdv', wg, kc, vc)
        n_new = decay[..., None] * n + jnp.einsum('bhs,bhsd->bhd', wg, kc)
        return (C_new, n_new, m_new), h

    state, hs = lax.scan(step, state, (chunks(q), chunks(k), chunks(v), chunks(log_i), chunks(log_f)))
    return jnp.moveaxis(hs, 0, 2).reshape(B, H, T, dv), state

def mlstm_bidirectional(q, k, v, li, lf, qc, kc, vc, lic, lfc):
    B, H, _, dk = q.shape
    dv = v.shape[-1]
    state0 = (jnp.zeros((B, H, dk, dv), jnp.float32), jnp.zeros((B, H, dk), jnp.float32),
              jnp.full((B, H), M_INIT, jnp.float32))
    outs_l, outs_c = [], []
    for d in range(2):
        rev = (lambda a: jnp.flip(a, axis=2)) if d == 1 else (lambda a: a)
        hc_d, st = mlstm_chunk_scan(rev(qc), rev(kc), rev(vc), rev(lic[d]), rev(lfc[d]), state0)
        hl_d, _ = mlstm_chunk_scan(rev(q), rev(k), rev(v), rev(li[d]), rev(lf[d]), st)
        outs_l.append(rev(hl_d))
        outs_c.append(rev(hc_d))
    return outs_l[0] + outs_l[1], outs_c[0] + outs_c[1]

def mlstm_output(h, o_raw, norm_g):
    h = jnp.swapaxes(h, 1, 2)
    h = h * lax.rsqrt(jnp.mean(h * h, axis=-1, keepdims=True) + EPS)
    B, T = h.shape[:2]
    return (h.reshape(B, T, M_WIDTH).astype(o_raw.dtype) * norm_g) * jax.nn.sigmoid(o_raw)

def merge_branches(branches, gate_raw, w_branch, w_out):
    B, T, _ = gate_raw.shape
    g = jax.nn.sigmoid(gate_raw.reshape(B, T, N_BRANCH, D_MODEL))
    y = g[:, :, 0] * (branches[0] @ w_branch[0])
    for i in range(1, N_BRANCH):
        y = y + g[:, :, i] * (branches[i] @ w_branch[i])
    return y @ w_out

def token_mixer(h, hc, cos, sin, w_in, m_conv_w, m_conv_b, m_gate_b, m_norm_g, g_qnorm, g_knorm,
                w_sink, n_rel_bias, w_branch, w_out, need_ctx):
    B, S, _ = h.shape
    C = hc.shape[1]
    (mq, mk, mv, mo, mif, gq, gk, gv, wq, wk, wv, nq, nk, nv, gate) = split_projection(h @ w_in)
    (mqc, mkc, mvc, moc, mifc, gqc, gkc, gvc, wqc, wkc, wvc, nqc, nkc, nvc, gatec) = split_projection(hc @ w_in)

    a_q, a_k, a_v, a_li, a_lf = mlstm_inputs(mq, mk, mv, mif, m_conv_w, m_conv_b, m_gate_b)
    ac_q, ac_k, ac_v, ac_li, ac_lf = mlstm_inputs(mqc, mkc, mvc, mifc, m_conv_w, m_conv_b, m_gate_b)
    h_lat, h_ctx = mlstm_bidirectional(a_q, a_k, a_v, a_li, a_lf, ac_q, ac_k, ac_v, ac_li, ac_lf)
    out_a = mlstm_output(h_lat, mo, m_norm_g)

    b_q = apply_rope(rms_norm(to_heads(gq, G_HEADS), g_qnorm), cos, sin)
    b_k = apply_rope(rms_norm(to_heads(gk, G_KV_HEADS), g_knorm), cos, sin)
    b_v = to_heads(gv, G_KV_HEADS)
    bc_q = rms_norm(to_heads(gqc, G_HEADS), g_qnorm)
    bc_k = rms_norm(to_heads(gkc, G_KV_HEADS), g_knorm)
    bc_v = to_heads(gvc, G_KV_HEADS)
    out_b = global_attention(b_q, jnp.concatenate([b_k, bc_k], axis=1),
                             jnp.concatenate([b_v, bc_v], axis=1)).reshape(B, S, -1)

    c_q = apply_rope(to_heads(wq, W_HEADS), cos, sin)
    c_k = apply_rope(to_heads(wk, W_KV_HEADS), cos, sin)
    c_v = to_heads(wv, W_KV_HEADS)
    cc_q, cc_k, cc_v = to_heads(wqc, W_HEADS), to_heads(wkc, W_KV_HEADS), to_heads(wvc, W_KV_HEADS)
    out_c = window_attention(c_q, c_k, c_v, cc_k, cc_v, w_sink).reshape(B, S, -1)

    d_q, d_k, d_v = to_heads(nq, N_HEADS), to_heads(nk, N_HEADS), to_heads(nv, N_HEADS)
    dc_q, dc_k, dc_v = to_heads(nqc, N_HEADS), to_heads(nkc, N_HEADS), to_heads(nvc, N_HEADS)
    out_d = neighbourhood_attention(d_q, d_k, d_v, dc_k, dc_v, n_rel_bias).reshape(B, S, -1)

    y = merge_branches([out_a, out_b, out_c, out_d], gate, w_branch, w_out)
    yc = None
    if need_ctx:
        oc_a = mlstm_output(h_ctx, moc, m_norm_g)
        oc_b = ctx_attention(bc_q, bc_k, bc_v).reshape(B, C, -1)
        oc_c = ctx_attention(cc_q, cc_k, cc_v, w_sink).reshape(B, C, -1)
        oc_d = ctx_attention(dc_q, dc_k, dc_v).reshape(B, C, -1)
        yc = merge_branches([oc_a, oc_b, oc_c, oc_d], gatec, w_branch, w_out)
    return y, yc

def moe_ffn(t, w_router, router_bias, e_gate, e_up, e_down):
    T, D = t.shape
    scores = jax.nn.sigmoid((t @ w_router).astype(jnp.float32))
    sel = (scores + router_bias.astype(jnp.float32)).reshape(T, N_GROUPS, EXPERTS_PER_GROUP)
    group_score = lax.top_k(sel, TOP_K)[0].sum(axis=-1)
    grp = jnp.argmax(group_score, axis=-1)
    in_group = jnp.take_along_axis(sel, grp[:, None, None], axis=1)[:, 0]
    _, local = lax.top_k(in_group, TOP_K)
    expert = grp[:, None] * EXPERTS_PER_GROUP + local
    w = jnp.take_along_axis(scores, expert, axis=1)
    w = w / w.sum(axis=-1, keepdims=True)

    n_assign = T * TOP_K
    e_flat = expert.reshape(-1)
    tok = jnp.repeat(jnp.arange(T, dtype=jnp.int32), TOP_K)
    w_flat = w.reshape(-1)
    order = jnp.argsort(e_flat)
    e_s, tok_s, w_s = e_flat[order], tok[order], w_flat[order]
    counts = jnp.bincount(e_flat, length=N_EXPERTS)
    starts = jnp.cumsum(counts) - counts
    padded = ((counts + MOE_BLOCK - 1) // MOE_BLOCK) * MOE_BLOCK
    pends = jnp.cumsum(padded)
    pstarts = pends - padded
    dest = pstarts[e_s] + (jnp.arange(n_assign) - starts[e_s])
    nblk = -(-(n_assign + N_EXPERTS * (MOE_BLOCK - 1)) // MOE_BLOCK)
    cap = nblk * MOE_BLOCK
    slot_tok = jnp.full((cap,), T, dtype=jnp.int32).at[dest].set(tok_s)
    slot_w = jnp.zeros((cap,), jnp.float32).at[dest].set(w_s)
    blk_e = jnp.minimum(jnp.searchsorted(pends, jnp.arange(nblk) * MOE_BLOCK, side='right'), N_EXPERTS - 1)
    t_pad = jnp.concatenate([t, jnp.zeros((1, D), t.dtype)], axis=0)
    xs = t_pad[slot_tok].reshape(nblk, MOE_BLOCK, D)

    def expert_block(args):
        xb, e = args
        hmid = jax.nn.silu(xb @ e_gate[e]) * (xb @ e_up[e])
        return hmid @ e_down[e]

    ys = lax.map(expert_block, (xs, blk_e)).reshape(cap, D)
    out = jnp.zeros((T + 1, D), ys.dtype).at[slot_tok].add(ys * slot_w[:, None].astype(ys.dtype))
    return out[:T]

def setup_inputs(seed: int = 0) -> dict:
    key = jax.random.key(seed)
    ks = jax.random.split(key, 32)
    f32 = jnp.float32
    L, D = DEPTH, D_MODEL

    def nrm(k, shape, scale):
        return jax.random.normal(k, shape, f32) * scale

    gate_base = jnp.array([-1.0, 3.0], f32).reshape(1, 1, 2, 1)
    return {
        'x': nrm(ks[0], (BATCH, SEQ, D), 1.0),
        'c': nrm(ks[1], (BATCH, D), 1.0),
        'ctx': nrm(ks[2], (BATCH, CTX_LEN, D), 1.0),
        'c_ctx': nrm(ks[3], (D,), 1.0),
        'w_mod': nrm(ks[4], (L, D, 6 * D), 0.5 * D ** -0.5),
        'b_mod': nrm(ks[5], (L, 6 * D), 0.02),
        'norm1_g': 1.0 + nrm(ks[6], (L, D), 0.05),
        'norm2_g': 1.0 + nrm(ks[7], (L, D), 0.05),
        'w_in': nrm(ks[8], (L, D, N_PROJ), D ** -0.5),
        'm_conv_w': nrm(ks[9], (L, CONV_K, 2 * M_WIDTH), CONV_K ** -0.5),
        'm_conv_b': nrm(ks[10], (L, 2 * M_WIDTH), 0.02),
        'm_gate_b': gate_base + nrm(ks[11], (L, 2, 2, M_HEADS), 0.2),
        'm_norm_g': 1.0 + nrm(ks[12], (L, M_WIDTH), 0.05),
        'g_qnorm': 1.0 + nrm(ks[13], (L, HEAD_DIM), 0.05),
        'g_knorm': 1.0 + nrm(ks[14], (L, HEAD_DIM), 0.05),
        'w_sink': nrm(ks[15], (L, W_HEADS), 0.5),
        'n_rel_bias': nrm(ks[16], (L, N_HEADS, 2 * NB_ROWS - 1, 2 * NB_COLS - 1), 0.5),
        'w_branch': nrm(ks[17], (L, N_BRANCH, BRANCH_WIDTH, D), BRANCH_WIDTH ** -0.5),
        'w_out': nrm(ks[18], (L, D, D), D ** -0.5),
        'w_router': nrm(ks[19], (D, N_EXPERTS), D ** -0.5),
        'router_bias': nrm(ks[20], (N_EXPERTS,), 0.01),
        'e_gate': nrm(ks[21], (L, N_EXPERTS, D, D_EXPERT), D ** -0.5),
        'e_up': nrm(ks[22], (L, N_EXPERTS, D, D_EXPERT), D ** -0.5),
        'e_down': nrm(ks[23], (L, N_EXPERTS, D_EXPERT, D), D_EXPERT ** -0.5),
        'final_g': 1.0 + nrm(ks[24], (D,), 0.05),
    }

def reference(x, c, ctx, c_ctx, w_mod, b_mod, norm1_g, norm2_g, w_in, m_conv_w, m_conv_b, m_gate_b,
              m_norm_g, g_qnorm, g_knorm, w_sink, n_rel_bias, w_branch, w_out, w_router, router_bias,
              e_gate, e_up, e_down, final_g):
    B, S, D = x.shape
    cos, sin = axial_rope_tables(S)
    xc = ctx
    for l in range(DEPTH):
        need_ctx = l < DEPTH - 1
        mod = jax.nn.silu(c) @ w_mod[l] + b_mod[l]
        sh1, sc1, ga1, sh2, sc2, ga2 = jnp.split(mod[:, None, :], 6, axis=-1)
        modc = jax.nn.silu(c_ctx) @ w_mod[l] + b_mod[l]
        csh1, csc1, cga1, csh2, csc2, cga2 = jnp.split(modc, 6)

        h = rms_norm(x, norm1_g[l]) * (1 + sc1) + sh1
        hc = rms_norm(xc, norm1_g[l]) * (1 + csc1) + csh1
        y, yc = token_mixer(h, hc, cos, sin, w_in[l], m_conv_w[l], m_conv_b[l], m_gate_b[l], m_norm_g[l],
                            g_qnorm[l], g_knorm[l], w_sink[l], n_rel_bias[l], w_branch[l], w_out[l], need_ctx)
        x = x + ga1 * y
        h2 = rms_norm(x, norm2_g[l]) * (1 + sc2) + sh2
        tokens = h2.reshape(B * S, D)
        if need_ctx:
            xc = xc + cga1 * yc
            hc2 = rms_norm(xc, norm2_g[l]) * (1 + csc2) + csh2
            tokens = jnp.concatenate([tokens, hc2.reshape(-1, D)], axis=0)
        f = moe_ffn(tokens, w_router, router_bias, e_gate[l], e_up[l], e_down[l])
        x = x + ga2 * f[:B * S].reshape(B, S, D)
        if need_ctx:
            xc = xc + cga2 * f[B * S:].reshape(B, -1, D)
    return rms_norm(x, final_g)


_drawn_inputs = setup_inputs


def setup_inputs(seed=0):
    import zlib

    import numpy as np

    out = dict(_drawn_inputs(seed))
    spreads = {}
    factors = {'m_conv_b': 12.215,
     'g_qnorm': 3.029,
     'g_knorm': 2.696,
     'w_sink': 30.399,
     'n_rel_bias': 3.141}
    for name, (base, spread) in spreads.items():
        noise = np.random.default_rng([zlib.crc32(name.encode()), seed]).standard_normal(out[name].shape)
        drawn = base * np.exp(spread * noise) if base else spread * noise
        out[name] = __import__('jax').numpy.asarray(drawn.astype(out[name].dtype))
    for name, factor in factors.items():
        out[name] = (out[name] * factor).astype(out[name].dtype)
    return out
```

```python
from contextlib import ExitStack

import numpy as np

import concourse.bass as bass
from concourse import mybir

F32 = mybir.dt.float32
I32 = mybir.dt.int32
U32 = mybir.dt.uint32
ALU = mybir.AluOpType
ACT = mybir.ActivationFunctionType
AX = mybir.AxisListType

P = 128
D = 1024
SEQ = 256
CTX = 256
TOK = SEQ + CTX
L = 2
GRID_W = 64
HD = 64
MD = 128
MH = 4
KT_D = D // P
EXPERTS = 32
GROUPS = 4
PER_GROUP = EXPERTS // GROUPS
DE = 512
EPS = 1e-6
NEG = -1e30
RING = 6
SLOT = 4096
N_DENSE = 2
HALF = 64
NB_ROWS, NB_COLS = 8, 16
REL_W = 2 * NB_COLS - 1
REL_H = 2 * NB_ROWS - 1

WIDTHS = (("mq", 512), ("mk", 512), ("mv", 512), ("mo", 512), ("mif", 16), ("gq", 512), ("gk", 128), ("gv", 128),
          ("wq", 512), ("wk", 128), ("wv", 128), ("nq", 512), ("nk", 512), ("nv", 512), ("gate", 4096))
COL = {}
_at = 0
for _n, _w in WIDTHS:
    COL[_n] = _at
    _at += _w
N_PROJ = _at

CAP = (96, 64)
N_PAR = 16 * (4 + L * 8)
N_TOK = (TOK, SEQ)
N_BLK = tuple(-(-N_TOK[l] // CAP[l]) for l in range(L))

CONST_COLS = {}
_at = 0
for _n, _w in (("ident", P), ("from_here", P), ("up_to_here", P), ("before", P), ("ones", P), ("fwd", 3 * P),
               ("bwd", 3 * P), ("colmask", GRID_W), ("cos", 64), ("sin", 64), ("expert", EXPERTS),
               ("falling", EXPERTS), ("gfalling", GROUPS)):
    CONST_COLS[_n] = (_at, _at + _w)
    _at += _w
N_CONST = _at


def shape_constants():
    c = np.zeros((P, N_CONST), np.float32)

    def put(name, value):
        a, b = CONST_COLS[name]
        c[:, a:b] = value

    p = np.arange(P)[:, None]
    f = np.arange(P)[None, :]
    put("ident", p == f)
    put("from_here", f >= p)
    put("up_to_here", f <= p)
    put("before", p < f)
    put("ones", 1.0)
    zero, full = np.zeros((P, P)), np.full((P, P), NEG)
    put("fwd", np.concatenate([zero, np.where(f <= p, 0.0, NEG), full], 1))
    put("bwd", np.concatenate([full, np.where(f >= p, 0.0, NEG), zero], 1))
    col = np.arange(P) % GRID_W
    start = np.clip(col - NB_COLS // 2, 0, GRID_W - NB_COLS)[:, None]
    k = np.arange(GRID_W)[None, :]
    put("colmask", np.where((k >= start) & (k < start + NB_COLS), 0.0, NEG)[:, ::-1])
    t = np.arange(SEQ)
    n_freq = HD // 4
    inv = np.float32(10000.0) ** (-np.arange(n_freq, dtype=np.float32) / np.float32(n_freq))
    ang = np.concatenate([(t // GRID_W).astype(np.float32)[:, None] * inv,
                          (t % GRID_W).astype(np.float32)[:, None] * inv], 1).astype(np.float32)
    put("cos", np.cos(ang).reshape(2, P, 32).transpose(1, 0, 2).reshape(P, 64))
    put("sin", np.sin(ang).reshape(2, P, 32).transpose(1, 0, 2).reshape(P, 64))
    put("expert", np.arange(EXPERTS))
    put("falling", EXPERTS - np.arange(EXPERTS))
    put("gfalling", GROUPS - np.arange(GROUPS))
    tok = np.stack([np.arange(4)[None, :] * rows(l) + np.arange(P)[:, None] for l in range(L)], 1).astype(np.int32)
    return c, tok


BRANCHES = "ABCD"
HEADS = {"A": MH, "B": 8, "C": 8, "D": 8}


def q_tiles(l):
    return 4 if l < L - 1 else 2


def rows(l):
    return P if l < L - 1 else HALF


def plan_dense():
    first, n = {}, 0
    for l in range(L):
        qt = q_tiles(l)
        for name, count in (("mod_a", 4), ("ht", 8), ("mq", 4), ("mk", 4), ("mv", 4), ("mif", 4), ("cum", 4),
                            ("cb", 8), ("mo", qt), ("otA", qt), ("mergeA", 16),
                            ("gq", qt), ("gkv", 4), ("qtB", qt), ("ktB", 1), ("otB", qt), ("mergeB", 16),
                            ("wq", qt), ("wkv", 4), ("qtC", qt), ("ktC", 1), ("otC", qt), ("mergeC", 16),
                            ("nq", 4), ("nk", 4), ("nv", 4), ("otD", qt), ("mergeD", 16),
                            ("mod_b", 8), ("out", 8), ("h2t", 8), ("router", 4), ("rank", 5)):
            first[l, name] = n
            n += count
    return first


def plan_items():
    items, n = {}, 0
    for l in range(L):
        for b in BRANCHES:
            todo = [(h, t) for h in range(HEADS[b]) for t in range(q_tiles(l))]
            items[l, b] = (n, todo)
            n += len(todo)
    return items


def hybrid_moe_kernel(nc, ins, out):
    G = plan_dense()
    ITEMS = plan_items()
    ctx = ExitStack()
    with ctx:
        def sb(name, shape, dt=F32):
            return ctx.enter_context(nc.sbuf_tensor(name, shape, dt))

        def sem(name):
            return ctx.enter_context(nc.semaphore(name))

        ring = sb("ring", [P, RING, SLOT])
        X = sb("X", [P, 4, D])
        HT = sb("HT", [P, KT_D, TOK])
        consts = sb("consts", [P, N_CONST])
        tokid = sb("tokid", [P, L, 4], I32)
        craw = sb("craw", [P, 2, KT_D])
        csil = sb("csil", [P, 2, KT_D])
        w_if = sb("w_if", [P, L, KT_D, 16])
        gate_b = sb("gate_b", [P, L, 16])
        conv_w = sb("conv_w", [P, L, 3, 8])
        conv_b = sb("conv_b", [P, L, 8])
        qk_g = sb("qk_g", [P, L, 2, HD])
        m_norm = sb("m_norm", [P, L, 512])
        sink = sb("sink", [P, L, 8])
        nsink = sb("nsink", [P, L, 8])
        w_router = sb("w_router", [P, KT_D, EXPERTS])
        r_bias = sb("r_bias", [P, EXPERTS])
        small = sb("small", [P, 256])
        SCR = 4096 + 8192 + 3584
        scr = sb("scr", [P, SCR])

        def const(name):
            a, b = CONST_COLS[name]
            return consts[:, a:b]

        ident, ones = const("ident"), const("ones")
        MG = scr[:, 0:4096].rearrange("p (k n) -> p k n", k=KT_D)
        HTOK = scr[:, 0:4096].rearrange("p (t n) -> p t n", t=4)
        BR0 = 4096

        def br(a, n):
            return scr[:, BR0 + a:BR0 + a + n]

        QT = br(0, 2048).rearrange("p (j n) -> p j n", j=4)
        OT = QT
        KT = br(2048, 2048).rearrange("p (j n) -> p j n", j=4)
        KT1 = br(2048, 512)
        V = br(4096, 2048).rearrange("p (t n) -> p t n", t=4)
        KV = br(4096, 1024).rearrange("p (t n) -> p t n", t=4)
        O = br(6144, 2048).rearrange("p (t n) -> p t n", t=4)
        WK = 8192
        CBS = br(WK, 2048).rearrange("p (b d n) -> p b d n", b=2, d=2)
        DW = scr[:, 0:2048].rearrange("p (b d n) -> p b d n", b=2, d=2)
        A_P = scr[:, 2048:3072].rearrange("p (b n) -> p b n", b=2)
        A_PT = scr[:, 3072:4096].rearrange("p (b n) -> p b n", b=2)
        A_TMP = DW[:, 0, 0, :]
        SGO = br(WK, 2048).rearrange("p (t n) -> p t n", t=4)
        PB = br(WK, 1024).rearrange("p (b n) -> p b n", b=2)
        PTB = br(WK + 1024, 1024).rearrange("p (b n) -> p b n", b=2)
        EB = br(WK + 2048, 1536).rearrange("p (h n) -> p h n", h=4)
        RT = br(WK + 2048, 1024).rearrange("p (a n) -> p a n", a=4)
        SGM = br(2048, 1024).rearrange("p (b n) -> p b n", b=2)
        TMP = br(3072, 512)
        MODA = br(0, 2048)
        G1 = br(2048, 1024)
        MODB = br(6144, 3072)
        G2 = br(9216, 1024)
        CS = {"mod_a": br(3072, 1024).rearrange("p (k m) -> p k m", k=KT_D),
              "mod_b": br(4096, 1024).rearrange("p (k m) -> p k m", k=KT_D)}
        GA2 = br(10240, 1024)
        XE = br(0, 2048).rearrange("p (b n) -> p b n", b=2)
        XT = br(2048, 1536)
        SG = br(3584, 384)
        HID = br(3968, 768).rearrange("p (b n) -> p b n", b=2)
        YS = br(4736, 2048).rearrange("p (b n) -> p b n", b=2)
        RTR = br(6784, 2400)
        idx_all = sb("idx_all", [P, L, EXPERTS], I32)
        idx = sb("idx", [P, 2], I32)
        zeros_i = sb("zeros_i", [P, EXPERTS], I32)
        OVA = HT[:, :, :].rearrange("p k n -> p (k n)")
        OVB = scr[:, 0:4096]
        dest_i = sb("dest_i", [P, L, 8], I32)
        cnt_i = sb("cnt_i", [1, L, EXPERTS + 1], I32)

        ss = small[:, 0:4]
        rstd = small[:, 4:8]
        hss = small[:, 8:40]
        hrs = small[:, 40:72]
        ifb = sb("ifb", [P, 4, 16])
        fx = small[:, 72:104].rearrange("p (t c) -> p t c", t=4)
        lf = small[:, 104:136].rearrange("p (t c) -> p t c", t=4)
        cc = sb("cc", [P, 4, 8])
        bb = sb("bb", [P, 4, 8])
        fabs = small[:, 136:168].rearrange("p (t c) -> p t c", t=4)
        fe = small[:, 168:200].rearrange("p (t c) -> p t c", t=4)
        mx = sb("mx", [P, 2, 2, 4])
        guard = sb("guard", [P, 2, 2])
        den = sb("den", [P, 2])
        rden = sb("rden", [P, 2])
        nm = sb("nm", [P, 4])
        nms = sb("nms", [P, 4])
        rsum = sb("rsum", [P, 4])
        esink = sb("esink", [P, 4])
        wn = sb("wn", [P, L, 2, 4])

        ps = [ctx.enter_context(nc.psum_tensor(f"bank{i}", [P, 512], F32)) for i in range(8)]

        h2_dram = [nc.dram_tensor(f"h2_{l}", [4 * rows(l), D], F32, kind="Internal").ap() for l in range(L)]
        slot_dram = [nc.dram_tensor(f"slot_{l}", [N_BLK[l] * CAP[l] * EXPERTS, 1], I32, kind="Internal").ap()
                     for l in range(L)]
        ys_dram = [nc.dram_tensor(f"ys_{l}", [N_BLK[l] * CAP[l] * EXPERTS, D], F32, kind="Internal").ap()
                   for l in range(L)]

        c_loaded = sem("c_loaded")
        x_loaded = sem("x_loaded")
        passed = sem("passed")
        par_loaded = sem("par_loaded")
        w_full = [sem(f"w_full{i}") for i in range(RING)]
        dense_full = sem("dense_full")
        dense_free = [sem(f"dense_free{i}") for i in range(N_DENSE)]
        dve_step = sem("dve_step")
        act_step = sem("act_step")
        pool_step = sem("pool_step")
        csil_ready = sem("csil_ready")
        cs_ready = sem("cs_ready")
        mod_loaded = sem("mod_loaded")
        ss_ready = sem("ss_ready")
        var_ready = sem("var_ready")
        std_ready = sem("std_ready")
        h_ready = sem("h_ready")
        act_evac = sem("act_evac")
        conv_ready = sem("conv_ready")
        fabs_ready = sem("fabs_ready")
        fln_ready = sem("fln_ready")
        lf_ready = sem("lf_ready")
        cc_ready = sem("cc_ready")
        cb_ready = sem("cb_ready")
        cb_used = sem("cb_used")
        dve_half = sem("first_direction_ready")
        s_full = sem("s_full")
        mx_ready = sem("mx_ready")
        w_ready = sem("w_ready")
        p_ready = sem("p_ready")
        pt_full = sem("pt_full")
        pt_ready = [sem(f"pt_ready{i}") for i in range(2)]
        o_full = sem("o_full")
        o_done = sem("o_done")
        o_ready = sem("o_ready")
        hss_ready = sem("hss_ready")
        hstd_ready = sem("hstd_ready")
        rot_ready = sem("rot_ready")
        sgo_ready = sem("sgo_ready")
        bias_loaded = sem("bias_loaded")
        bias_used = sem("bias_used")
        sgm_ready = sem("sgm_ready")
        mg_done = sem("mg_done")
        x_mid = sem("x_mid")
        h2_stored = sem("h2_stored")
        score_ready = sem("score_ready")
        oh_ready = sem("oh_ready")
        dest_ready = sem("dest_ready")
        slots_zero = sem("slots_zero")
        slots_cleared = sem("slots_cleared")
        slots_written = sem("slots_written")
        idx_loaded = sem("idx_loaded")
        xe_full = [sem(f"xe_full{i}") for i in range(2)]
        xe_used = sem("xe_used")
        xt_full = sem("xt_full")
        xt_ready = sem("xt_ready")
        g_full = sem("g_full")
        u_full = sem("u_full")
        sg_ready = sem("sg_ready")
        hid_ready = sem("hid_ready")
        y_full = sem("y_full")
        y_done = sem("y_done")
        ys_stored = [sem(f"ys_stored{i}") for i in range(2)]
        ov_zero = [sem(f"ov_zero{i}") for i in range(L)]
        ov_cleared = [sem(f"ov_cleared{i}") for i in range(L)]
        ovx = sem("ov_x")
        ovi = sem("ov_idx")
        ov_w = [sem(f"ov_w{i}") for i in range(3)]
        ov_xt = sem("ov_xt_full")
        ov_xtr = sem("ov_xt_ready")
        ov_g = sem("ov_g_full")
        ov_u = sem("ov_u_full")
        ov_sg = sem("ov_sg_ready")
        ov_hid = sem("ov_hid_ready")
        ov_y = sem("ov_y_full")
        ov_yd = sem("ov_y_done")
        ov_st = sem("ov_stored")
        yg_full = [sem(f"yg_full{i}") for i in range(2)]
        yg_used = sem("yg_used")
        x_done = sem("x_done")
        fin_ready = sem("fin_ready")
        out_stored = sem("out_stored")

        blocks = []
        BLOCK = {}

        def add_block(key, src, width, done):
            BLOCK[key] = len(blocks)
            blocks.append((src, width, done))

        def kview(ap, a, b):
            return ap.rearrange("(k p) n -> p k n", p=P)[:, :, a:b]

        for l in range(L):
            qt = q_tiles(l)

            def upto(stage, n, l=l):
                return (dense_full, G[l, stage] + n)

            w_in, w_mod = ins["w_in"][l], ins["w_mod"][l]
            for n in range(4):
                add_block((l, "mod", n), kview(w_mod, n * 512, n * 512 + 512), 512, upto("mod_a", n + 1))
            for name, n in (("mq", 4), ("mk", 4), ("mv", 4), ("mo", qt)):
                add_block((l, name), kview(w_in, COL[name], COL[name] + 512), 512, upto(name, n))
            for i, b in enumerate(BRANCHES):
                if b in "BC":
                    q, kv = ("gq", "gk") if b == "B" else ("wq", "wk")
                    add_block((l, q), kview(w_in, COL[q], COL[q] + 512), 512, upto(q, qt))
                    add_block((l, kv), kview(w_in, COL[kv], COL[kv] + 256), 256, upto(kv[0] + "kv", 4))
                if b == "D":
                    for name in ("nq", "nk", "nv"):
                        add_block((l, name), kview(w_in, COL[name], COL[name] + 512), 512, upto(name, 4))
                wb = ins["w_branch"][l, i].rearrange("(k p) n -> p k n", p=P)
                add_block((l, "wb", i), wb, D, upto("merge" + b, 16))
                for n in range(2):
                    a = COL["gate"] + i * D + n * 512
                    add_block((l, "gate", i, n), kview(w_in, a, a + 512), 512, upto("merge" + b, 8 * n + 8))
            for n in range(4, 12):
                add_block((l, "mod", n), kview(w_mod, n * 512, n * 512 + 512), 512, upto("mod_b", n - 3))
            for n in range(2):
                add_block((l, "out", n), kview(ins["w_out"][l], n * 512, n * 512 + 512), 512, upto("out", 7 + n))
            BLOCK[l, "experts"] = len(blocks)
            for e in range(EXPERTS):
                n = l * EXPERTS + e + 1
                for c, (src, s, v) in enumerate(((ins["e_gate"][l, e], g_full, n), (ins["e_up"][l, e], u_full, n),
                                                 (ins["e_down"][l, e], y_full, 2 * n))):
                    width = 512 if c < 2 else D
                    blocks.append((src.rearrange("(k p) n -> p k n", p=P), width, (s, v)))

        def slot_view(n, width):
            k = SLOT // 512 if width <= 512 else SLOT // width
            return ring[:, n % RING, 0:k * width].rearrange("p (k n) -> p k n", k=k)

        def weights(eng, key):
            n = BLOCK[key]
            eng.wait_ge(w_full[n % RING], 16 * (n // RING + 1))
            return slot_view(n, blocks[n][1])

        def parity_count(a, par):
            return (a + 1 - par) // 2

        def wait_alone(eng, *waits):
            for s, v in waits:
                eng.wait_ge(s, v)
            eng.sem_inc(passed, 1)

        class Steps:

            def __init__(self, eng, s):
                self.eng, self.s, self.n = eng, s, 0

            def __call__(self, ins_):
                ins_.then_inc(self.s, 1)
                self.n += 1
                self.eng.wait_ge(self.s, self.n)

        def dense_wait(eng, g):
            eng.wait_ge(dense_full, g + 1)
            return ps[g % N_DENSE]

        block = ctx.enter_context(nc.Block())

        @block.sync
        def _(sp):
            sp.dma_start(craw[:, 0, :], ins["c"]).then_inc(c_loaded, 16)
            sp.dma_start(craw[:, 1, :], ins["c_ctx"]).then_inc(c_loaded, 16)
            sp.dma_start(X[0:HALF, :, :], ins["x"][0].rearrange("(t p) d -> p t d", p=HALF)).then_inc(x_loaded, 16)
            sp.dma_start(X[HALF:P, :, :], ins["ctx"][0].rearrange("(t p) d -> p t d", p=HALF)).then_inc(x_loaded, 16)

            def issue(n):
                src, width, _done = blocks[n]
                if n >= RING:
                    s, v = blocks[n - RING][2]
                    sp.wait_ge(s, v)
                sp.dma_start(slot_view(n, width), src).then_inc(w_full[n % RING], 16)

            n = 0
            for l in range(L):
                first = BLOCK[l, "experts"]
                while n < first + RING:
                    issue(n)
                    n += 1
                laps = EXPERTS * 3 // RING
                with sp.Fori(1, laps) as i:
                    for j in range(2):
                        e_done = l * EXPERTS + 2 * i - 1 + j
                        for c, (w, s, v) in enumerate((("e_gate", g_full, e_done), ("e_up", u_full, e_done),
                                                       ("e_down", y_full, 2 * e_done))):
                            sp.wait_ge(s, v)
                            src = ins[w][l, bass.ds(2 * i + j, 1)].rearrange("a (k p) n -> p (a k) n", p=P)
                            m = first + 3 * j + c
                            sp.dma_start(slot_view(m, 512 if c < 2 else D), src).then_inc(w_full[m % RING], 16)
                n = first + 3 * EXPERTS
            sp.wait_ge(fin_ready, 4)
            sp.dma_start(out[0].rearrange("(t p) d -> p t d", p=HALF), HTOK[0:HALF, :, :]).then_inc(out_stored, 16)
            sp.wait_ge(out_stored, 16)

        @block.gpsimd
        def _(pool):
            step = Steps(pool, pool_step)
            n_ov = pool.alloc_register("pool_overflows")
            pool.reg_mov(n_ov, 0)
            n_par = 0

            def load_modulation(l):
                pool.dma_start(MODA, ins["b_mod"][l, 0:2 * D].partition_broadcast(P)).then_inc(mod_loaded, 16)
                pool.dma_start(G1, ins["norm1_g"][l].partition_broadcast(P)).then_inc(mod_loaded, 16)

            def par(dst, src):
                pool.dma_start(dst, src).then_inc(par_loaded, 16)
                return 16

            load_modulation(0)
            n_par += par(consts[:, :], ins["consts"])
            n_par += par(tokid[:, :, :], ins["tokid"])
            n_par += par(w_router[:, :, :], ins["w_router"])
            n_par += par(r_bias[:, :], ins["router_bias"].partition_broadcast(P))
            for l in range(L):
                n_par += par(w_if[:, l], ins["w_if"][l])
                n_par += par(gate_b[:, l, :], ins["m_gate_b"][l].rearrange("a b c -> (a b c)").partition_broadcast(P))
                n_par += par(conv_w[:, l], ins["m_conv_w"][l])
                n_par += par(conv_b[:, l, :], ins["m_conv_b"][l])
                n_par += par(qk_g[:, l, 0, :], ins["g_qnorm"][l].partition_broadcast(P))
                n_par += par(qk_g[:, l, 1, :], ins["g_knorm"][l].partition_broadcast(P))
                n_par += par(m_norm[:, l, :], ins["m_norm_g"][l].partition_broadcast(P))
                n_par += par(sink[:, l, :], ins["w_sink"][l].partition_broadcast(P))
            assert n_par == N_PAR

            pool.memset(zeros_i[:, :], 0).then_inc(slots_zero, 1)
            pool.wait_ge(slots_zero, 1)
            for l in range(L):
                table = slot_dram[l].rearrange("(b r e) o -> r b (e o)", r=CAP[l], e=EXPERTS)
                for b in range(N_BLK[l]):
                    pool.dma_start(table[:, b, :], zeros_i[0:CAP[l], :]).then_inc(slots_cleared, 16)

            gathered = [0, 0]
            for l in range(L):
                PN = rows(l)
                if l:
                    pool.wait_ge(x_done, 4 * l)
                    load_modulation(l)

                rel = ins["n_rel_bias"]
                for hh in range(2):
                    if hh == 0:
                        pool.wait_ge(dense_full, G[l, "nv"] + 4)
                    else:
                        pool.wait_ge(bias_used, l + 1)
                    for half in range(2):
                        for h in range(4):
                            off = ((l * 8 + hh * 4 + h) * REL_H + (4 + 1 - half)) * REL_W + NB_COLS - GRID_W
                            src = bass.AP(rel.tensor, rel.offset + off, [[1, GRID_W], [REL_W, 6], [1, GRID_W]])
                            dst = EB[half * HALF:half * HALF + HALF, h, :].rearrange("p (r c) -> p r c", r=6)
                            pool.dma_start(dst, src).then_inc(bias_loaded, 16)

                pool.wait_ge(dense_full, G[l, "otD"] + q_tiles(l))
                pool.dma_start(MODB, ins["b_mod"][l, 2 * D:5 * D].partition_broadcast(P)).then_inc(mod_loaded, 16)
                pool.dma_start(GA2, ins["b_mod"][l, 5 * D:6 * D].partition_broadcast(P)).then_inc(mod_loaded, 16)
                pool.dma_start(G2, ins["norm2_g"][l].partition_broadcast(P)).then_inc(mod_loaded, 16)

                for t in range(4):
                    pool.wait_ge(h_ready, 8 * l + 4 + t + 1)
                    pool.dma_start(h2_dram[l][t * PN:t * PN + PN, :], HTOK[0:PN, t, :]).then_inc(h2_stored, 16)
                pool.wait_ge(dest_ready, l + 1)
                pool.wait_ge(slots_cleared, 16 * sum(N_BLK))
                for k in range(2):
                    for t in range(4):
                        pool.indirect_dma_start(
                            slot_dram[l], bass.IndirectOffsetOnAxis(dest_i[0:PN, l, 4 * k + t:4 * k + t + 1].bitcast(U32), 0),
                            tokid[0:PN, l, t:t + 1], None).then_inc(slots_written, 16)
                pool.wait_ge(slots_written, 128 * (l + 1))
                pool.wait_ge(h2_stored, 64 * (l + 1))
                cap = CAP[l]
                pool.dma_start(idx_all[0:cap, l, :], slot_dram[l][0:cap * EXPERTS, :].rearrange(
                    "(r e) o -> r (e o)", e=EXPERTS)).then_inc(idx_loaded, 16)
                pool.wait_ge(idx_loaded, 16 * (l + 1))

                base = step.n
                with pool.Fori(0, EXPERTS // 2) as i:
                    for j in range(2):
                        pool.wait_ge(xe_used, (2 + EXPERTS) * l + 2 * i + j + 1)
                        pool.tensor_copy(idx[0:cap, j:j + 1], idx_all[0:cap, l, bass.ds(2 * i + j, 1)]).then_inc(pool_step, 1)
                        wait_alone(pool, (pool_step, base + 2 * i + j + 1))
                        pool.indirect_dma_start(XE[0:cap, j, :], None, h2_dram[l],
                                                bass.IndirectOffsetOnAxis(idx[0:cap, j:j + 1].bitcast(U32), 0)
                                                ).then_inc(xe_full[j], 16)
                step.n = base + EXPERTS

                most = pool.value_load(cnt_i[0:1, l, EXPERTS:EXPERTS + 1], min_val=0, max_val=TOK)
                for j in range(2):
                    pool.wait_ge(ys_stored[j], 16 + 16 * (l + 1) * EXPERTS // 2)
                def fetch_outputs(rows_):
                    for t in range(4):
                        for k in range(2):
                            if t >= 2:
                                pool.wait_ge(x_done, 4 * l + t - 1)
                            at = dest_i[0:PN, l, 4 * k + t:4 * k + t + 1].bitcast(U32)
                            pool.indirect_dma_start((XE, YS)[k][0:PN, t % 2, :], None, rows_,
                                                    bass.IndirectOffsetOnAxis(at, 0)).then_inc(yg_full[t % 2], 16)

                with pool.If(most > cap):
                    pool.memset(XE[:, 0, :], 0.0).then_inc(ov_zero[l], 1)
                    pool.wait_ge(ov_zero[l], 1)
                    n_rows = (N_BLK[l] - 1) * cap * EXPERTS // P
                    pool.dma_start(ys_dram[l][cap * EXPERTS:, :].rearrange("(a p) d -> p a d", p=P),
                                   XE[:, 0:1, :].to_broadcast([P, n_rows, D])).then_inc(ov_cleared[l], 16)
                    pool.wait_ge(ov_cleared[l], 16)
                    with pool.Fori(1, N_BLK[l]) as b:
                        with pool.Fori(0, EXPERTS) as e:
                            have = pool.value_load(cnt_i[0:1, l, bass.ds(e, 1)], min_val=0, max_val=TOK)
                            with pool.If(have > b * cap):
                                n = pool.snap(n_ov, min_val=0, max_val=4096)
                                row = b * (cap * EXPERTS) + e
                                slots = slot_dram[l].rearrange("(r e) o -> r (e o)", e=EXPERTS)
                                pool.dma_start(idx[0:cap, 0:1], slots[bass.ds(b * cap, cap), bass.ds(e, 1)],
                                               allow_slow_non_contiguous=True).then_inc(ovi, 16)
                                wait_alone(pool, (ovi, 16 * n + 16))
                                pool.indirect_dma_start(XE[0:cap, 0, :], None, h2_dram[l],
                                                        bass.IndirectOffsetOnAxis(idx[0:cap, 0:1].bitcast(U32), 0)
                                                        ).then_inc(ovx, 16)
                                for c, w in enumerate(("e_gate", "e_up", "e_down")):
                                    if c == 2:
                                        wait_alone(pool, (ov_g, n + 1))
                                    dst = (OVA, OVB, OVA)[c].rearrange("p (k n) -> p k n", k=8 if c < 2 else 4)
                                    src = ins[w][l, bass.ds(e, 1)].rearrange("a (k p) n -> p (a k) n", p=P)
                                    pool.dma_start(dst, src).then_inc(ov_w[c], 16)
                                wait_alone(pool, (ov_yd, n + 1))
                                ysv = ys_dram[l].rearrange("(r e) d -> r e d", e=EXPERTS)
                                pool.dma_start(ysv[bass.ds(b * cap, cap), bass.ds(e, 1), :],
                                               YS[0:cap, 0:1, :]).then_inc(ov_st, 16)
                                pool.wait_ge(ov_st, 16 * n + 16)
                                pool.reg_add(n_ov, n_ov, 1)

                    fetch_outputs(ys_dram[l])
                with pool.Else():
                    fetch_outputs(ys_dram[l][0:cap * EXPERTS, :])
            pool.wait_ge(x_done, 4 * L)
            pool.dma_start(G1, ins["final_g"].partition_broadcast(P)).then_inc(mod_loaded, 16)

        @block.scalar
        def _(act):
            step = Steps(act, act_step)
            n_ov = act.alloc_register("act_overflows")
            act.reg_mov(n_ov, 0)

            def evac(g, dst, src=None, func=ACT.Copy, done=act_evac, view=None):
                bank = dense_wait(act, g)
                src_ = src(bank)
                act.activation(dst, src_, func).then_inc(dense_free[g % N_DENSE], 1)

            act.wait_ge(c_loaded, 32)
            act.activation(csil[:, :, :], craw[:, :, :], ACT.Silu).then_inc(csil_ready, 1)
            act.wait_ge(x_loaded, 32)
            for l in range(L):
                PN = rows(l)
                qt = q_tiles(l)
                NQ = qt * P

                def norm_sums(which, pn):
                    for t in range(4):
                        act.activation(HTOK[0:pn, t, :], X[0:pn, t, :], ACT.Square,
                                       accum_out=ss[0:pn, t:t + 1]).then_inc(ss_ready, 1)
                    act.wait_ge(var_ready, which)
                    act.activation(ss[0:pn, :], ss[0:pn, :], ACT.Sqrt).then_inc(std_ready, 1)

                if l:
                    act.wait_ge(x_done, 4 * l)
                norm_sums(2 * l + 1, P)
                for t in range(4):
                    for hf in range(2):
                        dst = HT[:, 4 * hf:4 * hf + 4, :].rearrange("p k (s t c) -> p k s t c", s=2, t=4)[:, :, :, t, :]
                        evac(G[l, "ht"] + 2 * t + hf, dst,
                             lambda b: b[:, :].rearrange("p (k s c) -> p k s c", k=4, s=2))
                for n, (T_, cols) in enumerate([(QT[:, j, 0:NQ], j) for j in range(4)] + [(KT[:, j, :], j) for j in range(4)]):
                    act.wait_ge(conv_ready, 8 * l + n + 1)
                    act.activation(T_, T_, ACT.Silu).then_inc(act_evac, 1)
                for t in range(4):
                    evac(G[l, "mv"] + t, V[:, t, :], lambda b: b[:, :])
                if l == 0:
                    act.wait_ge(par_loaded, N_PAR)
                act.wait_ge(fabs_ready, l + 1)
                step(act.activation(fe, fabs, ACT.Exp, scale=-1.0))
                act.activation(fe, fe, ACT.Ln, bias=1.0).then_inc(fln_ready, 1)

                def pt_evac(a, w):
                    act.wait_ge(pt_full, a + 1)
                    dst = A_PT[:, a % 2, :]
                    if a >= 2:
                        act.wait_ge(o_full, a - 1)
                    act.activation(dst[:, 0:w], ps[6 + a % 2][:, 0:w], ACT.Copy).then_inc(pt_ready[a % 2], 1)

                a0, todo = ITEMS[l, "A"]
                last_evac = None
                for i, (h, q) in enumerate(todo):
                    a = a0 + i
                    if q == 0:
                        for d in range(2):
                            g = G[l, "cb"] + 2 * h + d
                            if h >= 2:
                                act.wait_ge(cb_used, MH * l + h - 1)
                            bank = dense_wait(act, g)
                            act.activation(CBS[:, h % 2, d, :], bank[:, :], ACT.Copy).then_inc(dense_free[g % N_DENSE], 1)
                            act.wait_ge(dense_free[g % N_DENSE], (g // N_DENSE + 1))
                        act.sem_inc(cb_ready, 1)
                    lat = q < 2
                    own = 0 if lat else 256
                    act.wait_ge(mx_ready, a + 1)
                    for d in range(2):
                        act.activation(DW[:, i % 2, d, own:own + 256], DW[:, i % 2, d, own:own + 256], ACT.Exp,
                                       bias=mx[:, i % 2, d, 3:4])
                        if lat:
                            act.activation(DW[:, i % 2, d, 256:512], CBS[:, h % 2, d, 256:512], ACT.Exp,
                                           bias=mx[:, i % 2, d, 3:4])
                        last = act.activation(guard[:, i % 2, d:d + 1], bb[:, q, 4 * d + h:4 * d + h + 1], ACT.Exp,
                                              bias=mx[:, i % 2, d, 3:4], scale=-1.0)
                    last.then_inc(w_ready, 1)
                    if last_evac is not None:
                        pt_evac(*last_evac)
                    last_evac = (a, 512 if lat else 256)
                pt_evac(*last_evac)

                act.wait_ge(hss_ready, 2 * l + 1)
                act.activation(hss[:, 0:4 * qt], hss[:, 0:4 * qt], ACT.Sqrt).then_inc(hstd_ready, 1)
                for t in range(qt):
                    g = G[l, "mo"] + t
                    bank = dense_wait(act, g)
                    act.activation(SGO[:, t, :], bank[:, :], ACT.Sigmoid).then_inc(dense_free[g % N_DENSE], 1)
                    act.wait_ge(dense_free[g % N_DENSE], (g // N_DENSE + 1))
                act.sem_inc(sgo_ready, 1)

                def out_transposed(b):
                    for t in range(qt):
                        evac(G[l, "ot" + b] + t, OT[:, :, t * P:t * P + P],
                             lambda b_: b_[:, :].rearrange("p (k c) -> p k c", k=4))

                def merge(b, i):
                    for ft in range(8):
                        n = 32 * l + 8 * i + ft
                        if n >= 2:
                            act.wait_ge(mg_done, n - 1)
                        g = G[l, "merge" + b] + 2 * ft
                        bank = dense_wait(act, g)
                        act.activation(SGM[:, ft % 2, 0:NQ], bank[:, 0:NQ], ACT.Sigmoid).then_inc(dense_free[g % N_DENSE], 1)
                        act.wait_ge(dense_free[g % N_DENSE], g // N_DENSE + 1)
                        act.sem_inc(sgm_ready, 1)
                    act.wait_ge(mg_done, 32 * l + 8 * i + 8)

                def attention(b):
                    a0, todo = ITEMS[l, b]
                    def tail(a, w):
                        if a % 2:
                            act.wait_ge(pt_full, a + 1)
                            act.wait_ge(o_full, a - 1)
                            act.activation(PTB[:, 1, 0:w], ps[7][:, 0:w], ACT.Copy).then_inc(pt_ready[1], 1)
                    for i, (h, q) in enumerate(todo):
                        a = a0 + i
                        par = a % 2
                        lo = 0 if q < 2 else 256
                        act.wait_ge(mx_ready, a + 1)
                        act.wait_ge(pt_full, a - 1)
                        if b == "C":
                            act.activation(esink[:, a % 4:a % 4 + 1], sink[:, l, h:h + 1], ACT.Exp, bias=nms[:, a % 4:a % 4 + 1])
                        act.activation(PB[:, par, 0:512 - lo], ps[4 + par][:, lo:512], ACT.Exp, bias=nms[:, a % 4:a % 4 + 1],
                                       scale=0.125, accum_out=rsum[:, a % 4:a % 4 + 1]).then_inc(p_ready, 1)
                        if i:
                            q1 = todo[i - 1][1]
                            tail(a - 1, 512 if q1 < 2 else 256)
                    tail(a0 + len(todo) - 1, 512 if todo[-1][1] < 2 else 256)

                out_transposed("A")
                merge("A", 0)
                for n, b in ((1, "B"), (2, "C")):
                    q_, kv_ = ("gq", "gkv") if b == "B" else ("wq", "wkv")
                    for t in range(qt):
                        evac(G[l, q_] + t, O[:, t, :].rearrange("p (j s c) -> p j s c", j=4, s=2),
                             lambda b_: b_[:, :].rearrange("p (s j c) -> p j s c", s=2, j=4))
                    for t in range(4):
                        evac(G[l, kv_] + t, KV[:, t, :], lambda b_: b_[:, 0:256])
                    if b == "B":
                        act.wait_ge(hss_ready, 2 * l + 2)
                        act.activation(small[:, 8:48], small[:, 8:48], ACT.Sqrt).then_inc(hstd_ready, 1)
                    for t in range(qt):
                        evac(G[l, "qt" + b] + t, QT[:, :, t * P:t * P + P],
                             lambda b_: b_[:, :].rearrange("p (k c) -> p k c", k=4))
                    evac(G[l, "kt" + b], KT1, lambda b_: b_[:, :])
                    attention(b)
                    out_transposed(b)
                    merge(b, n)
                for j in range(4):
                    evac(G[l, "nq"] + j, QT[:, j, 0:NQ], lambda b_: b_[:, 0:NQ])
                for j in range(4):
                    evac(G[l, "nk"] + j, KT[:, j, :], lambda b_: b_[:, :])
                for t in range(4):
                    evac(G[l, "nv"] + t, V[:, t, :], lambda b_: b_[:, :])
                attention("D")
                out_transposed("D")
                merge("D", 3)

                act.wait_ge(x_mid, l + 1)
                norm_sums(2 * l + 2, PN)
                for t in range(4):
                    for hf in range(2):
                        evac(G[l, "h2t"] + 2 * t + hf, HT[:, 4 * hf:4 * hf + 4, t * PN:t * PN + PN],
                             lambda b_: b_[:, 0:4 * PN].rearrange("p (k c) -> p k c", k=4))
                for t in range(4):
                    g = G[l, "router"] + t
                    bank = dense_wait(act, g)
                    act.activation(RTR[0:PN, 32 * t:32 * t + 32], bank[0:PN, 0:32], ACT.Sigmoid).then_inc(dense_free[g % N_DENSE], 1)
                    act.wait_ge(dense_free[g % N_DENSE], g // N_DENSE + 1)
                act.sem_inc(score_ready, 1)

                cap = CAP[l]
                eb = EXPERTS * l

                hw = 4 * cap
                ysv = ys_dram[l].rearrange("(r e) d -> r e d", e=EXPERTS)
                act.wait_ge(dense_full, G[l, "rank"] + 5)
                act.sem_inc(xe_used, 2)
                if l == 0:
                    for j in range(2):
                        act.sem_inc(ys_stored[j], 16)
                with act.Fori(0, EXPERTS // 2) as i:
                    for j in range(2):
                        n = eb + 2 * i + j + 1
                        act.wait_ge(g_full, n)
                        act.wait_ge(hid_ready, n)
                        act.activation(SG[:, 0:hw], ps[2][:, 0:hw], ACT.Silu).then_inc(sg_ready, 1)
                        act.wait_ge(y_done, n + 1)
                        act.dma_start(ysv[0:cap, bass.ds(2 * i + j, 1), :], YS[0:cap, j:j + 1, :]).then_inc(ys_stored[j], 16)
                most = act.value_load(cnt_i[0:1, l, EXPERTS:EXPERTS + 1], min_val=0, max_val=TOK)
                with act.If(most > cap):
                    with act.Fori(1, N_BLK[l]) as b:
                        with act.Fori(0, EXPERTS) as e:
                            have = act.value_load(cnt_i[0:1, l, bass.ds(e, 1)], min_val=0, max_val=TOK)
                            with act.If(have > b * cap):
                                n = act.snap(n_ov, min_val=0, max_val=4096)
                                act.wait_ge(ov_g, n + 1)
                                act.activation(SG[:, 0:hw], ps[2][:, 0:hw], ACT.Silu).then_inc(ov_sg, 1)
                                act.reg_add(n_ov, n_ov, 1)
            act.wait_ge(var_ready, 2 * L + 1)
            act.activation(ss[0:HALF, :], ss[0:HALF, :], ACT.Sqrt).then_inc(std_ready, 1)

        @block.tensor
        def _(pe):
            def dense(g, mms, last_inc=None):
                if g >= N_DENSE:
                    pe.wait_ge(dense_free[g % N_DENSE], g // N_DENSE)
                bank = ps[g % N_DENSE]
                ins_ = mms(bank)
                ins_.then_inc(dense_full, 1)

            def project_features(l, name, w, n_out, cols):
                for j in range(4):
                    def mms(bank):
                        for k in range(KT_D):
                            m = pe.matmul(bank[:, 0:cols], w[:, k, j * P:j * P + P], HT[:, k, 0:cols],
                                          start=k == 0, stop=k == KT_D - 1)
                        return m
                    dense(G[l, name] + j, mms)

            def project_tokens(l, name, w, n_tiles, width):
                for t in range(n_tiles):
                    def mms(bank):
                        for k in range(KT_D):
                            m = pe.matmul(bank[:, 0:width], HT[:, k, t * P:t * P + P], w[:, k, 0:width],
                                          start=k == 0, stop=k == KT_D - 1)
                        return m
                    dense(G[l, name] + t, mms)

            n_ov = pe.alloc_register("pe_overflows")
            pe.reg_mov(n_ov, 0)
            for l in range(L):
                PN = rows(l)
                qt = q_tiles(l)
                NQ = qt * P

                def modulation(stage, lo, hi):
                    cs = CS[stage]
                    pe.wait_ge(cs_ready, 2 * l + (1 if stage == "mod_a" else 2))
                    for n in range(lo, hi):
                        w = weights(pe, (l, "mod", n))
                        def mms(bank):
                            for k in range(KT_D):
                                m = pe.matmul(bank[:, :], cs[:, k, :], w[:, k, :], start=k == 0, stop=k == KT_D - 1)
                            return m
                        dense(G[l, stage] + n - lo, mms)

                def transposes(g, srcs, pn=P):
                    def mms(bank):
                        for k, s in enumerate(srcs):
                            m = pe.transpose(bank[:, k * pn:k * pn + pn], s, ident[0:pn, 0:pn])
                        return m
                    dense(g, mms)

                modulation("mod_a", 0, 4)
                if l == 0:
                    pe.wait_ge(par_loaded, N_PAR)
                for t in range(4):
                    pe.wait_ge(h_ready, 8 * l + t + 1)
                    for hf in range(2):
                        transposes(G[l, "ht"] + 2 * t + hf, [HTOK[:, t, (4 * hf + k) * P:(4 * hf + k + 1) * P] for k in range(4)])
                for g in range(G[l, "ht"] + 5, G[l, "ht"] + 8):
                    pe.wait_ge(dense_free[g % N_DENSE], g // N_DENSE + 1)

                project_features(l, "mq", weights(pe, (l, "mq")), 4, NQ)
                project_features(l, "mk", weights(pe, (l, "mk")), 4, TOK)
                project_tokens(l, "mv", weights(pe, (l, "mv")), 4, 512)
                project_tokens(l, "mif", w_if[:, l], 4, 16)
                pe.wait_ge(lf_ready, l + 1)
                for t in range(4):
                    def mms(bank):
                        for d, order in enumerate(((2, 3, 0, 1), (3, 2, 1, 0))):
                            upto = order[:order.index(t) + 1]
                            for s in upto:
                                tri = ones if s != t else (const("from_here"), const("up_to_here"))[d]
                                m = pe.matmul(bank[:, 4 * d:4 * d + 4], tri, lf[:, s, 4 * d:4 * d + 4],
                                              start=s == upto[0], stop=s == t)
                        return m
                    dense(G[l, "cum"] + t, mms)

                def spread(h):
                    for d in range(2):
                        def mms(bank):
                            for s in range(4):
                                m = pe.matmul(bank[:, s * P:s * P + P],
                                              cc[:, s, 4 * d + h:4 * d + h + 1].to_broadcast([P, P]), ident,
                                              start=True, stop=True)
                            return m
                        dense(G[l, "cb"] + 2 * h + d, mms)

                def attention(b):
                    a0, todo = ITEMS[l, b]
                    n = len(todo)

                    def scores(i):
                        h, q = todo[i]
                        a = a0 + i
                        lo = 0 if q < 2 else 256
                        if a >= 2:
                            pe.wait_ge(p_ready, a - 1)
                        bank = ps[4 + a % 2]
                        cols = slice(q * P, q * P + P)
                        if b == "A":
                            if q == 0:
                                spread(h)
                            lhsT, rhs = QT[:, h, cols], KT[:, h, lo:512]
                        elif b == "D":
                            s = (h % 2) * HD
                            lhsT, rhs = QT[s:s + HD, h // 2, cols], KT[s:s + HD, h // 2, lo:512]
                        else:
                            s = (h // 4) * HD
                            lhsT, rhs = QT[s:s + HD, h % 4, cols], KT1[s:s + HD, lo:512]
                        pe.matmul(bank[:, lo:512], lhsT, rhs, start=True, stop=True).then_inc(s_full, 1)

                    def turn(i):
                        h, q = todo[i]
                        a = a0 + i
                        pe.wait_ge(p_ready, a + 1)
                        if parity_count(a, a % 2):
                            pe.wait_ge(pt_ready[a % 2], parity_count(a, a % 2))
                        src = A_P[:, a % 2, :] if b == "A" else PB[:, a % 2, :]
                        nk = 4 if q < 2 else 2
                        for k in range(nk):
                            m = pe.transpose(ps[6 + a % 2][:, k * P:k * P + P], src[:, k * P:k * P + P], ident)
                        m.then_inc(pt_full, 1)

                    def values(i):
                        h, q = todo[i]
                        a = a0 + i
                        pe.wait_ge(pt_ready[a % 2], parity_count(a, a % 2) + 1)
                        if a >= 2:
                            pe.wait_ge(o_done, a - 1)
                        src = A_PT[:, a % 2, :] if b == "A" else PTB[:, a % 2, :]
                        tiles = range(4) if q < 2 else (2, 3)
                        width = MD if b == "A" else HD
                        dst = ps[2 + a % 2][:, 0:width]
                        for n_, s in enumerate(tiles):
                            if b in "AD":
                                v = V[:, s, h * width:(h + 1) * width]
                            else:
                                v = KV[:, s, P + (h // 4) * HD:P + (h // 4) * HD + HD]
                            m = pe.matmul(dst, src[:, n_ * P:n_ * P + P], v, start=n_ == 0, stop=n_ == len(tiles) - 1)
                        m.then_inc(o_full, 1)

                    for i in range(n + 2):
                        if i < n:
                            scores(i)
                        if 1 <= i <= n:
                            turn(i - 1)
                        if i >= 2:
                            values(i - 2)

                def out_transposed(b):
                    pe.wait_ge(o_ready, 4 * l + BRANCHES.index(b) + 1)
                    for t in range(qt):
                        transposes(G[l, "ot" + b] + t, [O[:, t, k * P:k * P + P] for k in range(4)])

                def evacuated(last):
                    for g in range(last - N_DENSE + 1, last + 1):
                        pe.wait_ge(dense_free[g % N_DENSE], g // N_DENSE + 1)

                def merge(b, i):
                    evacuated(G[l, "ot" + b] + qt - 1)
                    wb = weights(pe, (l, "wb", i))
                    for ft in range(8):
                        if ft % 4 == 0:
                            w = weights(pe, (l, "gate", i, ft // 4))
                        def gate(bank):
                            for k in range(KT_D):
                                m = pe.matmul(bank[:, 0:NQ], w[:, k, (ft % 4) * P:(ft % 4) * P + P], HT[:, k, 0:NQ],
                                              start=k == 0, stop=k == KT_D - 1)
                            return m
                        def value(bank):
                            for k in range(4):
                                m = pe.matmul(bank[:, 0:NQ], wb[:, k, ft * P:ft * P + P], OT[:, k, 0:NQ],
                                              start=k == 0, stop=k == 3)
                            return m
                        dense(G[l, "merge" + b] + 2 * ft, gate)
                        dense(G[l, "merge" + b] + 2 * ft + 1, value)

                pe.wait_ge(cc_ready, l + 1)
                pe.wait_ge(act_evac, 8 * (l + 1))
                evacuated(G[l, "mv"] + 3)
                attention("A")
                project_tokens(l, "mo", weights(pe, (l, "mo")), qt, 512)
                out_transposed("A")
                merge("A", 0)
                for n, b in ((1, "B"), (2, "C")):
                    q_, kv_ = ("gq", "gk") if b == "B" else ("wq", "wk")
                    project_tokens(l, q_, weights(pe, (l, q_)), qt, 512)
                    project_tokens(l, kv_[0] + "kv", weights(pe, (l, kv_)), 4, 256)
                    pe.wait_ge(rot_ready, 2 * l + n)
                    for t in range(qt):
                        transposes(G[l, "qt" + b] + t, [O[:, t, k * P:k * P + P] for k in range(4)])
                    transposes(G[l, "kt" + b], [KV[:, t, 0:P] for t in range(4)])
                    evacuated(G[l, "kt" + b])
                    attention(b)
                    out_transposed(b)
                    merge(b, n)
                project_features(l, "nq", weights(pe, (l, "nq")), 4, NQ)
                project_features(l, "nk", weights(pe, (l, "nk")), 4, TOK)
                project_tokens(l, "nv", weights(pe, (l, "nv")), 4, 512)
                evacuated(G[l, "nv"] + 3)
                attention("D")
                out_transposed("D")
                merge("D", 3)

                modulation("mod_b", 4, 12)
                pe.wait_ge(mg_done, 32 * (l + 1))
                wo = [weights(pe, (l, "out", n)) for n in range(2)]
                for t in range(4):
                    for n in range(2):
                        def mms(bank):
                            for k in range(KT_D):
                                m = pe.matmul(bank[0:PN, :], MG[:, k, t * PN:t * PN + PN], wo[n][:, k, :], start=k == 0, stop=k == KT_D - 1)
                            return m
                        dense(G[l, "out"] + 2 * t + n, mms)
                for t in range(4):
                    pe.wait_ge(h_ready, 8 * l + 4 + t + 1)
                    for hf in range(2):
                        transposes(G[l, "h2t"] + 2 * t + hf,
                                   [HTOK[0:PN, t, (4 * hf + k) * P:(4 * hf + k + 1) * P] for k in range(4)], PN)
                evacuated(G[l, "h2t"] + 7)
                for t in range(4):
                    def mms(bank):
                        for k in range(KT_D):
                            m = pe.matmul(bank[0:PN, 0:EXPERTS], HT[:, k, t * PN:t * PN + PN], w_router[:, k, :],
                                          start=k == 0, stop=k == KT_D - 1)
                        return m
                    dense(G[l, "router"] + t, mms)
                pe.wait_ge(oh_ready, l + 1)
                M = RTR[0:PN, 640:768].rearrange("p (t e) -> p t e", t=4)
                for t in range(4):
                    def mms(bank):
                        for s in range(t + 1):
                            tri = ones if s < t else const("before")
                            m = pe.matmul(bank[0:PN, 0:EXPERTS], tri[0:PN, 0:PN], M[:, s, :], start=s == 0, stop=s == t)
                        return m
                    dense(G[l, "rank"] + t, mms)
                def total(bank):
                    for s in range(4):
                        m = pe.matmul(bank[0:PN, 0:EXPERTS], ones[0:PN, 0:PN], M[:, s, :], start=s == 0, stop=s == 3)
                    return m
                dense(G[l, "rank"] + 4, total)
                evacuated(G[l, "rank"] + 4)

                cap = CAP[l]
                eb = EXPERTS * l
                first = BLOCK[l, "experts"]

                def turn_tokens(par, pn):
                    for k in range(KT_D):
                        m = pe.transpose(ps[k // 4][:, (k % 4) * cap:(k % 4) * cap + cap],
                                         XE[0:cap, par, k * P:k * P + P], ident[0:cap, 0:cap])
                    return m

                XTv = XT[:, 0:8 * cap].rearrange("p (k c) -> p k c", k=8)

                def hidden(bank, w):
                    for f in range(4):
                        for k in range(KT_D):
                            m = pe.matmul(ps[bank][:, f * cap:f * cap + cap], w[:, k, f * P:f * P + P], XTv[:, k, :],
                                          start=k == 0, stop=k == KT_D - 1)
                    return m

                def down(n, w, par):
                    hv = HID[:, par, 0:4 * cap].rearrange("p (f c) -> p f c", f=4)
                    for f in range(4):
                        m = pe.matmul(ps[4 + n][0:cap, :], hv[:, f, :], w[:, f, n * 512:n * 512 + 512],
                                      start=f == 0, stop=f == 3)
                    return m

                def gathered_turn(j, arrived_, n):
                    wait_alone(pe, (xe_full[j], arrived_), (xt_ready, n))
                    turn_tokens(j, cap).then_inc(xt_full, 1)

                def expert(i, j, next_too):
                    n = eb + 2 * i + j + 1
                    m0 = first + 3 * j
                    wv = [slot_view(m0 + c, 512 if c < 2 else D) for c in range(3)]

                    def arrived(c):
                        pe.wait_ge(w_full[(m0 + c) % RING], 16 * ((m0 + c) // RING + 1) + 16 * i)

                    pe.wait_ge(xt_full, n)
                    pe.sem_inc(xe_used, 1)
                    pe.wait_ge(xt_ready, n + 1)
                    arrived(0)
                    hidden(2, wv[0]).then_inc(g_full, 1)
                    arrived(1)
                    hidden(3, wv[1]).then_inc(u_full, 1)
                    if next_too:
                        gathered_turn(1 - j, 8 * eb + 16 * (i + j) + 16, n + 1)
                    arrived(2)
                    pe.wait_ge(hid_ready, n + 1)
                    pe.wait_ge(y_done, n)
                    for half in range(2):
                        down(half, wv[2], j).then_inc(y_full, 1)

                gathered_turn(0, 8 * eb + 16, eb + 1)
                with pe.Fori(0, EXPERTS // 2 - 1) as i:
                    for j in range(2):
                        expert(i, j, True)
                for j in range(2):
                    expert(EXPERTS // 2 - 1, j, j == 0)
                most = pe.value_load(cnt_i[0:1, l, EXPERTS:EXPERTS + 1], min_val=0, max_val=TOK)
                pe.wait_ge(y_done, eb + EXPERTS + 1)
                with pe.If(most > cap):
                    with pe.Fori(1, N_BLK[l]) as b:
                        with pe.Fori(0, EXPERTS) as e:
                            have = pe.value_load(cnt_i[0:1, l, bass.ds(e, 1)], min_val=0, max_val=TOK)
                            with pe.If(have > b * cap):
                                n = pe.snap(n_ov, min_val=0, max_val=4096)
                                wait_alone(pe, (ovx, 16 * n + 16))
                                turn_tokens(0, cap).then_inc(ov_xt, 1)
                                pe.wait_ge(ov_xtr, n + 1)
                                pe.wait_ge(ov_w[0], 16 * n + 16)
                                hidden(2, OVA.rearrange("p (k n) -> p k n", k=8)).then_inc(ov_g, 1)
                                pe.wait_ge(ov_w[1], 16 * n + 16)
                                hidden(3, OVB.rearrange("p (k n) -> p k n", k=8)).then_inc(ov_u, 1)
                                pe.wait_ge(ov_w[2], 16 * n + 16)
                                pe.wait_ge(ov_hid, n + 1)
                                w = OVA.rearrange("p (k n) -> p k n", k=4)
                                down(0, w, 0).then_inc(ov_y, 1)
                                down(1, w, 0).then_inc(ov_y, 1)
                                pe.wait_ge(ov_yd, n + 1)
                                pe.reg_add(n_ov, n_ov, 1)

        @block.vector
        def _(dve):
            step = Steps(dve, dve_step)
            n_ov = dve.alloc_register("dve_overflows")
            dve.reg_mov(n_ov, 0)

            def free(g, ins_):
                ins_.then_inc(dense_free[g % N_DENSE], 1)

            def free_step(g, ins_):
                ins_.then_inc(dense_free[g % N_DENSE], 1)
                dve.wait_ge(dense_free[g % N_DENSE], g // N_DENSE + 1)

            dve.wait_ge(csil_ready, 1)

            def spread_c(stage):
                for s in range(2):
                    dst = CS[stage][:, :, s * HALF:s * HALF + HALF]
                    last = dve.tensor_copy(dst, csil[:, s, :].unsqueeze(2).to_broadcast([P, KT_D, HALF]))
                last.then_inc(cs_ready, 1)

            for l in range(L):
                PN = rows(l)
                qt = q_tiles(l)
                NQ = qt * P

                def rms_factors(which, pn):
                    dve.wait_ge(ss_ready, 4 * which)
                    dve.tensor_scalar(ss[0:pn, :], ss[0:pn, :], 1.0 / D, EPS, ALU.mult, ALU.add).then_inc(var_ready, 1)
                    dve.wait_ge(std_ready, which)
                    step(dve.reciprocal(rstd[0:pn, :], ss[0:pn, :]))

                def modulated(pn, scale, shift):
                    for t in range(4):
                        step(dve.scalar_tensor_tensor(out=HTOK[0:pn, t, :], in0=X[0:pn, t, :], scalar=rstd[0:pn, t:t + 1],
                                                      in1=scale[0:pn, :], op0=ALU.mult, op1=ALU.mult))
                        dve.tensor_tensor(HTOK[0:pn, t, :], HTOK[0:pn, t, :], shift[0:pn, :], ALU.add).then_inc(h_ready, 1)

                spread_c("mod_a")
                dve.wait_ge(mod_loaded, 80 * l + 32)
                for n in range(4):
                    g = G[l, "mod_a"] + n
                    bank = dense_wait(dve, g)
                    free_step(g, dve.tensor_tensor(MODA[:, n * 512:n * 512 + 512], MODA[:, n * 512:n * 512 + 512], bank[:, :], ALU.add))
                step(dve.scalar_tensor_tensor(out=MODA[:, D:2 * D], in0=MODA[:, D:2 * D], scalar=1.0, in1=G1,
                                              op0=ALU.add, op1=ALU.mult))
                rms_factors(2 * l + 1, P)
                modulated(P, MODA[:, D:2 * D], MODA[:, 0:D])

                if l == 0:
                    dve.wait_ge(par_loaded, N_PAR)
                    step(dve.tensor_scalar(nsink[:, :, :], sink[:, :, :], -1.0, None, ALU.mult))
                for n in range(8):
                    T_ = (QT if n < 4 else KT)[:, n % 4, :]
                    segs = 2 if (n >= 4 or NQ == TOK) else 1
                    g = G[l, "mq"] + n
                    bank = dense_wait(dve, g)
                    w3 = segs * 256
                    def seg(ap, a, b_):
                        return ap[:, 0:w3].rearrange("p (s c) -> p s c", s=segs)[:, :, a:b_]
                    if n == 0:
                        dve.wait_ge(h_ready, 8 * l + 4)
                    step(dve.tensor_scalar(T_[:, 0:w3], bank[:, 0:w3], conv_w[:, l, 1, n:n + 1], conv_b[:, l, n:n + 1],
                                           ALU.mult, ALU.add))
                    step(dve.scalar_tensor_tensor(out=seg(T_, 1, 256), in0=seg(bank, 0, 255), scalar=conv_w[:, l, 0, n:n + 1],
                                                  in1=seg(T_, 1, 256), op0=ALU.mult, op1=ALU.add))
                    free_step(g, dve.scalar_tensor_tensor(out=seg(T_, 0, 255), in0=seg(bank, 1, 256),
                                                          scalar=conv_w[:, l, 2, n:n + 1], in1=seg(T_, 0, 255),
                                                          op0=ALU.mult, op1=ALU.add))
                    dve.sem_inc(conv_ready, 1)
                for t in range(4):
                    g = G[l, "mif"] + t
                    bank = dense_wait(dve, g)
                    free_step(g, dve.tensor_tensor(ifb[:, t, :], bank[:, 0:16], gate_b[:, l, :], ALU.add))
                gv = ifb[:, :, :].rearrange("p t (d g h) -> p t d g h", d=2, g=2)
                step(dve.tensor_copy(fx.rearrange("p t (d h) -> p t d h", d=2), gv[:, :, :, 1, :]))
                dve.scalar_tensor_tensor(out=fabs, in0=fx, scalar=-1.0, in1=fx, op0=ALU.mult, op1=ALU.max).then_inc(fabs_ready, 1)
                dve.wait_ge(fln_ready, l + 1)
                dve.scalar_tensor_tensor(out=lf, in0=fx, scalar=0.0, in1=fe, op0=ALU.min, op1=ALU.subtract).then_inc(lf_ready, 1)
                for t in range(4):
                    g = G[l, "cum"] + t
                    bank = dense_wait(dve, g)
                    step(dve.tensor_copy(bb[:, t, :], bank[:, 0:8]))
                    free_step(g, dve.tensor_tensor(cc[:, t, :].rearrange("p (d h) -> p d h", d=2), gv[:, t, :, 0, :],
                                                   bank[:, 0:8].rearrange("p (d h) -> p d h", d=2), ALU.subtract))
                dve.sem_inc(cc_ready, 1)

                def o_evac(a, dst, width, scale=None):
                    dve.wait_ge(o_full, a + 1)
                    src = ps[2 + a % 2][:, 0:width]
                    if scale is None:
                        dve.tensor_copy(dst, src).then_inc(o_done, 1)
                    else:
                        dve.tensor_scalar(dst, src, scale, None, ALU.mult).then_inc(o_done, 1)

                a0, todo = ITEMS[l, "A"]
                w_base = sum(len(ITEMS[m, "A"][1]) for m in range(l))

                def decay(i):
                    h, q = todo[i]
                    own = 0 if q < 2 else 256
                    if q == 0:
                        dve.wait_ge(cb_ready, MH * l + h + 1)
                    for d in range(2):
                        strip = const(("fwd", "bwd")[d])
                        at = P - (q % 2) * P
                        w_, m_ = DW[:, i % 2, d, :], mx[:, i % 2, d, :]
                        step(dve.tensor_tensor(w_[:, own:own + 256], CBS[:, h % 2, d, own:own + 256],
                                               strip[:, at:at + 256], ALU.add))
                        dve.tensor_reduce(m_[:, 0:1], w_[:, own:own + 256], AX.X, ALU.max)
                        src = CBS[:, h % 2, d, 256:512] if q < 2 else w_[:, 256:512]
                        step(dve.tensor_reduce(m_[:, 1:2], src, AX.X, ALU.max))
                        dve.tensor_reduce(m_[:, 3:4], m_[:, 0:2], AX.X, ALU.max, negate=True).then_inc(
                            mx_ready if d else dve_half, 1)
                    if q == qt - 1:
                        dve.sem_inc(cb_used, 1)

                decay(0)
                for i, (h, q) in enumerate(todo):
                    a = a0 + i
                    lo = 0 if q < 2 else 256
                    if i + 1 < len(todo):
                        decay(i + 1)
                    dve.wait_ge(s_full, a + 1)
                    dve.wait_ge(w_ready, w_base + i + 1)
                    w_ = DW[:, i % 2, :, :]
                    for d in range(2):
                        step(dve.scalar_tensor_tensor(out=w_[:, d, lo:512], in0=ps[4 + a % 2][:, lo:512], scalar=MD ** -0.5,
                                                      in1=w_[:, d, lo:512], op0=ALU.mult, op1=ALU.mult,
                                                      accum_out=den[:, d:d + 1]))
                        step(dve.scalar_tensor_tensor(out=rden[:, d:d + 1], in0=den[:, d:d + 1], scalar=-1.0,
                                                      in1=den[:, d:d + 1], op0=ALU.mult, op1=ALU.max))
                        step(dve.tensor_tensor(den[:, d:d + 1], rden[:, d:d + 1], guard[:, i % 2, d:d + 1], ALU.max))
                        step(dve.reciprocal(rden[:, d:d + 1], den[:, d:d + 1]))
                    if a >= 2:
                        dve.wait_ge(pt_full, a - 1)
                    p_ = A_P[:, a % 2, 0:512 - lo]
                    step(dve.tensor_scalar(p_, w_[:, 0, lo:512], rden[:, 0:1], None, ALU.mult))
                    dve.scalar_tensor_tensor(out=p_, in0=w_[:, 1, lo:512], scalar=rden[:, 1:2],
                                             in1=p_, op0=ALU.mult, op1=ALU.add).then_inc(p_ready, 1)
                    if i >= 2:
                        h1, q1 = todo[i - 2]
                        o_evac(a - 2, O[:, q1, h1 * MD:(h1 + 1) * MD], MD)
                for i in range(len(todo) - 2, len(todo)):
                    h1, q1 = todo[i]
                    o_evac(a0 + i, O[:, q1, h1 * MD:(h1 + 1) * MD], MD)
                dve.wait_ge(o_done, a0 + len(todo))
                for t in range(qt):
                    step(dve.tensor_tensor(A_TMP, O[:, t, :], O[:, t, :], ALU.mult))
                    step(dve.tensor_reduce(hss[:, 4 * t:4 * t + 4], A_TMP.rearrange("p (h c) -> p h c", h=4), AX.X, ALU.add))
                dve.tensor_scalar(hss[:, 0:4 * qt], hss[:, 0:4 * qt], 1.0 / MD, EPS, ALU.mult, ALU.add).then_inc(hss_ready, 1)
                dve.wait_ge(hstd_ready, 2 * l + 1)
                step(dve.reciprocal(hrs[:, 0:4 * qt], hss[:, 0:4 * qt]))
                dve.wait_ge(sgo_ready, l + 1)
                for t in range(qt):
                    for h in range(MH):
                        o_ = O[:, t, h * MD:(h + 1) * MD]
                        last = dve.scalar_tensor_tensor(out=o_, in0=o_, scalar=hrs[:, 4 * t + h:4 * t + h + 1],
                                                        in1=m_norm[:, l, h * MD:(h + 1) * MD], op0=ALU.mult, op1=ALU.mult)
                        step(last)
                    step(dve.tensor_tensor(O[:, t, :], O[:, t, :], SGO[:, t, :], ALU.mult))
                dve.sem_inc(o_ready, 1)

                def merge(b, i):
                    def mixed(ap):
                        ap = ap[:, 0:NQ]
                        return ap.rearrange("p (t s c) -> p t s c", t=4, s=2) if NQ == TOK else ap

                    def natural(ap):
                        ap = ap[:, 0:NQ]
                        return ap.rearrange("p (s t c) -> p t s c", t=4, s=2) if NQ == TOK else ap

                    for ft in range(8):
                        n = 32 * l + 8 * i + ft
                        g = G[l, "merge" + b] + 2 * ft + 1
                        bank = dense_wait(dve, g)
                        dve.wait_ge(sgm_ready, n + 1)
                        if i == 0:
                            free_step(g, dve.tensor_tensor(mixed(MG[:, ft, :]), natural(SGM[:, ft % 2, :]), natural(bank), ALU.mult))
                            dve.sem_inc(mg_done, 1)
                        else:
                            free_step(g, dve.tensor_tensor(TMP[:, 0:NQ], SGM[:, ft % 2, 0:NQ], bank[:, 0:NQ], ALU.mult))
                            dve.tensor_tensor(mixed(MG[:, ft, :]), mixed(MG[:, ft, :]), natural(TMP), ALU.add).then_inc(mg_done, 1)
                            dve.wait_ge(mg_done, n + 1)

                def attention(b):
                    a0, todo = ITEMS[l, b]

                    def tail(i):
                        h, q = todo[i]
                        a = a0 + i
                        w = 512 if q < 2 else 256
                        if a % 2 == 0:
                            dve.wait_ge(pt_full, a + 1)
                            dve.wait_ge(o_full, a - 1)
                            dve.tensor_copy(PTB[:, 0, 0:w], ps[6][:, 0:w]).then_inc(pt_ready[0], 1)

                    def fin(i):
                        h, q = todo[i]
                        a = a0 + i
                        par = a % 2
                        dve.wait_ge(p_ready, a + 1)
                        if b == "C":
                            step(dve.tensor_tensor(rsum[:, a % 4:a % 4 + 1], rsum[:, a % 4:a % 4 + 1], esink[:, a % 4:a % 4 + 1], ALU.add))
                        step(dve.reciprocal(rden[:, par:par + 1], rsum[:, a % 4:a % 4 + 1]))
                        o_evac(a, O[:, q, h * HD:(h + 1) * HD], HD, rden[:, par:par + 1])

                    for i, (h, q) in enumerate(todo):
                        a = a0 + i
                        par = a % 2
                        lo = 0 if q < 2 else 256
                        S = ps[4 + par]
                        dve.wait_ge(s_full, a + 1)
                        if q < 2 and b == "C":
                            strip = const("fwd")[:, 0:256] if q == 0 else const("bwd")[:, P:P + 256]
                            step(dve.tensor_tensor(S[:, 0:256], S[:, 0:256], strip, ALU.add))
                        if q < 2 and b == "D":
                            if h % 4 == 0 and q == 0:
                                hh = 2 * l + h // 4
                                dve.wait_ge(bias_loaded, 128 * (hh + 1))
                                for h_ in range(4):
                                    step(dve.scalar_tensor_tensor(
                                        out=EB[:, h_, :].rearrange("p (r c) -> p r c", r=6),
                                        in0=EB[:, h_, :].rearrange("p (r c) -> p r c", r=6), scalar=8.0,
                                        in1=const("colmask").unsqueeze(1).to_broadcast([P, 6, GRID_W]),
                                        op0=ALU.mult, op1=ALU.add))
                            at = (2 - 2 * q) * GRID_W
                            rows_ = S[:, 0:256].rearrange("p (r c) -> p r c", r=4)
                            bias = EB[:, h % 4, at:at + 256].rearrange("p (r c) -> p r c", r=4)[:, :, ::-1]
                            step(dve.tensor_tensor(rows_, rows_, bias, ALU.add))
                            if h == 3 and q == 1:
                                dve.sem_inc(bias_used, 1)
                        step(dve.tensor_reduce(nm[:, a % 4:a % 4 + 1], S[:, lo:512], AX.X, ALU.max, negate=True))
                        if b == "C":
                            last = dve.tensor_scalar(nms[:, a % 4:a % 4 + 1], nm[:, a % 4:a % 4 + 1], 0.125, nsink[:, l, h:h + 1],
                                                     ALU.mult, ALU.min)
                        else:
                            last = dve.tensor_scalar(nms[:, a % 4:a % 4 + 1], nm[:, a % 4:a % 4 + 1], 0.125, None, ALU.mult)
                        last.then_inc(mx_ready, 1)
                        if i >= 1:
                            tail(i - 1)
                        if i >= 2:
                            fin(i - 2)
                    n = len(todo)
                    tail(n - 1)
                    fin(n - 2)
                    fin(n - 1)
                    dve.wait_ge(o_done, a0 + n)
                    dve.sem_inc(o_ready, 1)

                def rope(x, c, s, nh):
                    xv = x.rearrange("p (h i two) -> p h i two", h=nh, two=2)
                    x0, x1 = xv[:, :, :, 0], xv[:, :, :, 1]
                    cb, sb_ = (a_.unsqueeze(1).to_broadcast([P, nh, 32]) for a_ in (c, s))
                    w = nh * 32
                    T_ = [RT[:, k, 0:w].rearrange("p (h i) -> p h i", h=nh) for k in range(4)]
                    dve.tensor_tensor(T_[0], x0, cb, ALU.mult)
                    dve.tensor_tensor(T_[1], x1, sb_, ALU.mult)
                    dve.tensor_tensor(T_[2], x0, sb_, ALU.mult)
                    step(dve.tensor_tensor(T_[3], x1, cb, ALU.mult))
                    dve.tensor_tensor(x0, T_[0], T_[1], ALU.subtract)
                    step(dve.tensor_tensor(x1, T_[2], T_[3], ALU.add))

                merge("A", 0)
                for n, b in ((1, "B"), (2, "C")):
                    kv0 = G[l, ("gkv", "wkv")[n - 1]]
                    for g in range(kv0 + 4 - N_DENSE, kv0 + 4):
                        dve.wait_ge(dense_free[g % N_DENSE], g // N_DENSE + 1)
                    parts = [(O[:, t, :], 8, t, 0) for t in range(qt)] + [(KV[:, t, 0:P], 2, t, 1) for t in range(4)]
                    if b == "B":
                        at = 0
                        sq = RT[:, :, :].rearrange("p a n -> p (a n)")
                        for x, nh, t, gi in parts:
                            step(dve.tensor_tensor(sq[:, 0:nh * HD], x, x, ALU.mult))
                            step(dve.tensor_reduce(small[:, 8 + at:8 + at + nh],
                                                   sq[:, 0:nh * HD].rearrange("p (h c) -> p h c", h=nh), AX.X, ALU.add))
                            at += nh
                        if at < 40:
                            step(dve.memset(small[:, 8 + at:48], 1.0))
                        dve.tensor_scalar(small[:, 8:48], small[:, 8:48], 1.0 / HD, EPS, ALU.mult, ALU.add).then_inc(hss_ready, 1)
                        dve.wait_ge(hstd_ready, 2 * l + 2)
                        step(dve.reciprocal(small[:, 8:48], small[:, 8:48]))
                        at = 0
                        for x, nh, t, gi in parts:
                            xv = x.rearrange("p (h c) -> p h c", h=nh)
                            step(dve.tensor_tensor(xv, xv, small[:, 8 + at:8 + at + nh].unsqueeze(2).to_broadcast([P, nh, HD]), ALU.mult))
                            step(dve.tensor_tensor(xv, xv, qk_g[:, l, gi, :].unsqueeze(1).to_broadcast([P, nh, HD]), ALU.mult))
                            at += nh
                    for x, nh, t, gi in parts:
                        if t < 2:
                            rope(x, const("cos")[:, 32 * t:32 * t + 32], const("sin")[:, 32 * t:32 * t + 32], nh)
                    dve.sem_inc(rot_ready, 1)
                    attention(b)
                    merge(b, n)
                attention("D")
                spread_c("mod_b")
                merge("D", 3)

                dve.wait_ge(mod_loaded, 80 * (l + 1))
                for n in range(8):
                    g = G[l, "mod_b"] + n
                    bank = dense_wait(dve, g)
                    dst = MODB[:, n * 512:n * 512 + 512] if n < 6 else GA2[:, (n - 6) * 512:(n - 6) * 512 + 512]
                    free_step(g, dve.tensor_tensor(dst, dst, bank[:, :], ALU.add))
                GA1, SH2, SC2 = (MODB[:, k * D:(k + 1) * D] for k in range(3))
                step(dve.scalar_tensor_tensor(out=SC2, in0=SC2, scalar=1.0, in1=G2, op0=ALU.add, op1=ALU.mult))
                for t in range(4):
                    for n in range(2):
                        g = G[l, "out"] + 2 * t + n
                        bank = dense_wait(dve, g)
                        cols = slice(n * 512, n * 512 + 512)
                        free_step(g, dve.tensor_tensor(TMP[0:PN, :], bank[0:PN, :], GA1[0:PN, cols], ALU.mult))
                        step(dve.tensor_tensor(X[0:PN, t, cols], X[0:PN, t, cols], TMP[0:PN, :], ALU.add))
                dve.sem_inc(x_mid, 1)
                rms_factors(2 * l + 2, PN)
                modulated(PN, SC2, SH2)

                def r4(at, n):
                    return RTR[0:PN, at:at + 4 * n].rearrange("p (t e) -> p t e", t=4)

                SCO, SEL, SELM, OH = r4(0, 32), r4(128, 32), r4(256, 32), (r4(384, 32), r4(512, 32))
                M, EQ, T8 = r4(640, 32), r4(768, 32), RTR[0:PN, 896:1024].rearrange("p (t g k) -> p t g k", t=4, g=4)
                GS, GE, GM, GN = r4(1024, 4), r4(1040, 4), r4(1056, 4), r4(1072, 4)
                m1, m2 = RTR[0:PN, 1088:1092], RTR[0:PN, 1092:1096]
                W = (RTR[0:PN, 1096:1100], RTR[0:PN, 1100:1104])
                WS = RTR[0:PN, 1104:1108]
                DF = RTR[0:PN, 1112:1120]
                RK = RTR[0:PN, 1120:1152]
                CF = RTR[0:PN, 1152:1185]

                def wide(a_, n):
                    return a_.unsqueeze(2).to_broadcast([PN, 4, n])

                def over(a_, n):
                    return a_[0:PN, :].unsqueeze(1).to_broadcast([PN, 4, n])

                def first_max(dst, src, eq, falling, n):
                    step(dve.tensor_reduce(m1, src, AX.X, ALU.max))
                    step(dve.tensor_tensor(eq, src, wide(m1, n), ALU.is_equal))
                    step(dve.tensor_tensor(eq, eq, over(falling, n), ALU.mult))
                    step(dve.tensor_reduce(m2, eq, AX.X, ALU.max))
                    step(dve.tensor_tensor(dst, eq, wide(m2, n), ALU.is_equal))

                dve.wait_ge(score_ready, l + 1)
                step(dve.tensor_tensor(SEL, SCO, over(r_bias, 32), ALU.add))
                for t in range(4):
                    for g_ in range(GROUPS):
                        last = dve.max(T8[:, t, g_, :], SEL[:, t, g_ * 8:g_ * 8 + 8])
                step(last)
                step(dve.tensor_tensor(GS, T8[:, :, :, 0], T8[:, :, :, 1], ALU.add))
                first_max(GM, GS, GE, const("gfalling"), 4)
                step(dve.tensor_scalar(GN, GM, -NEG, NEG, ALU.mult, ALU.add))
                bc8 = [RTR[0:PN, a_:a_ + 16].unsqueeze(2).to_broadcast([PN, 16, 8]) for a_ in (1056, 1072)]
                flat = [RTR[0:PN, a_:a_ + 128].rearrange("p (g k) -> p g k", k=8) for a_ in (128, 256)]
                step(dve.tensor_tensor(flat[1], flat[0], bc8[0], ALU.mult))
                step(dve.tensor_tensor(flat[1], flat[1], bc8[1], ALU.add))
                for k in range(2):
                    first_max(OH[k], SELM, EQ, const("falling"), 32)
                    step(dve.tensor_tensor(EQ, SCO, OH[k], ALU.mult))
                    step(dve.tensor_reduce(W[k], EQ, AX.X, ALU.add))
                    if k == 0:
                        step(dve.scalar_tensor_tensor(out=SELM, in0=OH[0], scalar=2 * NEG, in1=SELM, op0=ALU.mult, op1=ALU.add))
                dve.tensor_tensor(M, OH[0], OH[1], ALU.add).then_inc(oh_ready, 1)
                step(dve.tensor_tensor(WS, W[0], W[1], ALU.add))
                step(dve.reciprocal(WS, WS))
                for k in range(2):
                    step(dve.tensor_tensor(wn[0:PN, l, k, :], W[k], WS, ALU.mult))
                for t in range(4):
                    g = G[l, "rank"] + t
                    bank = dense_wait(dve, g)
                    free_step(g, dve.scalar_tensor_tensor(out=RK, in0=bank[0:PN, 0:32], scalar=float(EXPERTS),
                                                          in1=const("expert")[0:PN, :], op0=ALU.mult, op1=ALU.add))
                    for k in range(2):
                        step(dve.tensor_tensor(EQ[:, k, :], RK, OH[k][:, t, :], ALU.mult))
                        step(dve.tensor_reduce(DF[:, 4 * k + t:4 * k + t + 1], EQ[:, k, :], AX.X, ALU.add))
                g = G[l, "rank"] + 4
                bank = dense_wait(dve, g)
                free_step(g, dve.tensor_copy(CF[:, 0:32], bank[0:PN, 0:32]))
                step(dve.tensor_reduce(CF[:, 32:33], CF[:, 0:32], AX.X, ALU.max))
                step(dve.tensor_copy(cnt_i[0:1, l, :], CF[0:1, :]))
                dve.tensor_copy(dest_i[0:PN, l, :], DF).then_inc(dest_ready, 1)

                cap = CAP[l]
                eb = EXPERTS * l
                hw = 4 * cap

                def take_tokens(xt_done):
                    for hf in range(2):
                        last = dve.tensor_copy(XT[:, hf * hw:hf * hw + hw], ps[hf][:, 0:hw])
                    last.then_inc(xt_done, 1)

                def take_outputs(par, done):
                    for hf in range(2):
                        last = dve.tensor_copy(YS[0:cap, par, hf * 512:hf * 512 + 512], ps[4 + hf][0:cap, :])
                    last.then_inc(done, 1)

                if l == 0:
                    for s_ in (xt_ready, hid_ready, y_done):
                        dve.sem_inc(s_, 1)

                def expert(i, j, next_too):
                    n = eb + 2 * i + j + 1
                    dve.wait_ge(sg_ready, n)
                    dve.wait_ge(u_full, n)
                    dve.tensor_tensor(HID[:, j, 0:hw], SG[:, 0:hw], ps[3][:, 0:hw], ALU.mult).then_inc(hid_ready, 1)
                    if next_too:
                        dve.wait_ge(xt_full, n + 1)
                        take_tokens(xt_ready)
                    dve.wait_ge(y_full, 2 * n)
                    dve.wait_ge(ys_stored[j], 8 * eb + 16 * i + 16)
                    take_outputs(j, y_done)

                dve.wait_ge(xt_full, eb + 1)
                take_tokens(xt_ready)
                with dve.Fori(0, EXPERTS // 2 - 1) as i:
                    for j in range(2):
                        expert(i, j, True)
                for j in range(2):
                    expert(EXPERTS // 2 - 1, j, j == 0)
                most = dve.value_load(cnt_i[0:1, l, EXPERTS:EXPERTS + 1], min_val=0, max_val=TOK)
                with dve.If(most > cap):
                    with dve.Fori(1, N_BLK[l]) as b:
                        with dve.Fori(0, EXPERTS) as e:
                            have = dve.value_load(cnt_i[0:1, l, bass.ds(e, 1)], min_val=0, max_val=TOK)
                            with dve.If(have > b * cap):
                                n = dve.snap(n_ov, min_val=0, max_val=4096)
                                dve.wait_ge(ov_xt, n + 1)
                                take_tokens(ov_xtr)
                                dve.wait_ge(ov_sg, n + 1)
                                dve.wait_ge(ov_u, n + 1)
                                dve.tensor_tensor(HID[:, 0, 0:hw], SG[:, 0:hw], ps[3][:, 0:hw], ALU.mult).then_inc(ov_hid, 1)
                                dve.wait_ge(ov_y, 2 * n + 2)
                                take_outputs(0, ov_yd)
                                dve.reg_add(n_ov, n_ov, 1)

                for t in range(4):
                    dve.wait_ge(yg_full[t % 2], 32 * (2 * l + t // 2 + 1))
                    y0, y1 = XE[0:PN, t % 2, :], YS[0:PN, t % 2, :]
                    step(dve.tensor_scalar(y0, y0, wn[0:PN, l, 0, t:t + 1], None, ALU.mult))
                    step(dve.scalar_tensor_tensor(out=y0, in0=y1, scalar=wn[0:PN, l, 1, t:t + 1], in1=y0, op0=ALU.mult, op1=ALU.add))
                    dve.tensor_tensor(y0, y0, GA2[0:PN, :], ALU.mult).then_inc(yg_used, 1)
                    dve.wait_ge(yg_used, 4 * l + t + 1)
                    dve.tensor_tensor(X[0:PN, t, :], X[0:PN, t, :], y0, ALU.add).then_inc(x_done, 1)
                    dve.wait_ge(x_done, 4 * l + t + 1)
            for t in range(4):
                x = X[0:HALF, t, :]
                step(dve.tensor_tensor(HTOK[0:HALF, t, :], x, x, ALU.mult))
                step(dve.tensor_reduce(ss[0:HALF, t:t + 1], HTOK[0:HALF, t, :], AX.X, ALU.add))
            dve.tensor_scalar(ss[0:HALF, :], ss[0:HALF, :], 1.0 / D, EPS, ALU.mult, ALU.add).then_inc(var_ready, 1)
            dve.wait_ge(std_ready, 2 * L + 1)
            step(dve.reciprocal(rstd[0:HALF, :], ss[0:HALF, :]))
            dve.wait_ge(mod_loaded, 80 * L + 16)
            for t in range(4):
                dve.scalar_tensor_tensor(out=HTOK[0:HALF, t, :], in0=X[0:HALF, t, :], scalar=rstd[0:HALF, t:t + 1],
                                         in1=G1[0:HALF, :], op0=ALU.mult, op1=ALU.mult).then_inc(fin_ready, 1)


def columns(v):
    v = np.asarray(v)
    return np.ascontiguousarray(np.moveaxis(v.reshape(v.shape[:-1] + (v.shape[-1] // P, P)), -1, 0))


def row_tiles(w):
    w = np.asarray(w)
    return np.ascontiguousarray(np.swapaxes(w.reshape(w.shape[:-2] + (w.shape[-2] // P, P, w.shape[-1])), -3, -2))


_INS = ['x', 'c', 'ctx', 'c_ctx', 'w_mod', 'b_mod', 'norm1_g', 'norm2_g', 'w_in', 'm_conv_w', 'm_conv_b', 'm_gate_b',
        'm_norm_g', 'g_qnorm', 'g_knorm', 'w_sink', 'n_rel_bias', 'w_branch', 'w_out', 'w_router', 'router_bias',
        'e_gate', 'e_up', 'e_down', 'final_g', 'w_if']


def kernel(**inputs):
    import concourse.bacc as _bacc
    from concourse.bass_utils import run_bass_kernel_spmd as _run

    nc = _bacc.Bacc("TRN2", target_bir_lowering=False, num_devices=1)
    arrays, args = {}, {}
    consts, tokid = shape_constants()
    inputs["n_rel_bias"] = np.asarray(inputs["n_rel_bias"])[..., ::-1]
    inputs["w_if"] = row_tiles(np.asarray(inputs["w_in"])[:, :, COL["mif"]:COL["mif"] + 16])
    inputs["w_router"] = row_tiles(inputs["w_router"])
    inputs["c"], inputs["c_ctx"] = columns(np.asarray(inputs["c"])[0]), columns(inputs["c_ctx"])
    inputs["m_conv_w"] = np.ascontiguousarray(np.moveaxis(columns(inputs["m_conv_w"]), 1, 0))
    inputs["m_conv_b"] = np.ascontiguousarray(np.moveaxis(columns(inputs["m_conv_b"]), 1, 0))
    for name, a in [(n, np.ascontiguousarray(inputs[n])) for n in _INS] + [("consts", consts), ("tokid", tokid)]:
        arrays[f"in_{name}_dram"] = a
        args[name] = nc.dram_tensor(f"in_{name}_dram", a.shape, mybir.dt.from_np(a.dtype), kind="ExternalInput").ap()
    out = nc.dram_tensor("out_0_dram", (1, SEQ, D), F32, kind="ExternalOutput").ap()
    hybrid_moe_kernel(nc, args, out)
    r = _run(nc, [arrays], core_ids=[0])
    return r.results[0]["out_0_dram"]
```
